# Optimizing a Trainium2 kernel written in Bass

```python
import jax, jax.numpy as jnp
from jax import lax
import numpy as np

D_MODEL = 2048
BATCH = 1
SEQ = 512
DEPTH = 1

CHUNK = 64
D_MIX = D_MODEL
N_ATTN_HEADS = 16
HEAD_DIM = 64
D_ATTN = N_ATTN_HEADS * HEAD_DIM
D_RNN = D_MIX - D_ATTN
N_RNN_BLOCKS = 16
RNN_BLOCK = D_RNN // N_RNN_BLOCKS
RNN_CONV_W = 4
RG_C = 8.0
D_FF = 3 * D_MODEL
FFN_CONV_W = 3
Q_BLOCK = 128
EPS = 1e-6
D_IN = 3 * D_ATTN + N_ATTN_HEADS + 2 * D_RNN
SPLITS = (D_ATTN, 2 * D_ATTN, 3 * D_ATTN, 3 * D_ATTN + N_ATTN_HEADS, 3 * D_ATTN + N_ATTN_HEADS + D_RNN)

kernel_name = "fox_rglru_hymba_sandwich_block"

def rmsnorm(x, g):
    xf = x.astype(jnp.float32)
    y = xf * lax.rsqrt(jnp.mean(xf * xf, axis=-1, keepdims=True) + EPS)
    return (y * g.astype(jnp.float32)).astype(x.dtype)

def causal_dwconv(x, w, b):
    K = w.shape[0]
    S = x.shape[1]
    xp = jnp.pad(x, ((0, 0), (K - 1, 0), (0, 0)))
    return sum(xp[:, k:k + S] * w[k] for k in range(K)) + b

def forgetting_attention(q, k, v, log_f):
    S = q.shape[1]
    c = jnp.cumsum(log_f, axis=1).transpose(0, 2, 1)
    scale = HEAD_DIM ** -0.5
    outs = []
    for i in range(S // Q_BLOCK):
        q0 = i * Q_BLOCK
        kv_len = q0 + Q_BLOCK
        qb = q[:, q0:kv_len].astype(jnp.float32)
        kb = k[:, :kv_len].astype(jnp.float32)
        vb = v[:, :kv_len].astype(jnp.float32)
        logits = (jnp.einsum('bqhd,bkhd->bhqk', qb, kb) * scale
                  + c[:, :, q0:kv_len, None] - c[:, :, None, :kv_len])
        qpos = q0 + jnp.arange(Q_BLOCK)
        kpos = jnp.arange(kv_len)
        logits = jnp.where(kpos[None, :] <= qpos[:, None], logits, -jnp.inf)
        p = jax.nn.softmax(logits, axis=-1)
        outs.append(jnp.einsum('bhqk,bkhd->bqhd', p, vb).astype(v.dtype))
    return jnp.concatenate(outs, axis=1)

def rg_lru(x, w_a, b_a, w_x, b_x, lam):
    B, S, _ = x.shape
    xf = x.astype(jnp.float32)
    xb = xf.reshape(B, S, N_RNN_BLOCKS, RNN_BLOCK)
    r = jax.nn.sigmoid(jnp.einsum('bsni,nij->bsnj', xb, w_a.astype(jnp.float32)).reshape(B, S, D_RNN) + b_a)
    i_g = jax.nn.sigmoid(jnp.einsum('bsni,nij->bsnj', xb, w_x.astype(jnp.float32)).reshape(B, S, D_RNN) + b_x)
    log_a = -RG_C * r * jax.nn.softplus(-lam.astype(jnp.float32))
    a = jnp.exp(log_a)
    mult = jnp.sqrt(-jnp.expm1(2.0 * log_a))
    mult = jnp.where(jnp.arange(S)[None, :, None] == 0, 1.0, mult)
    bterm = mult * i_g * xf

    def combine(left, right):
        a1, b1 = left
        a2, b2 = right
        return a1 * a2, a2 * b1 + b2

    _, h = lax.associative_scan(combine, (a, bterm), axis=1)
    return h.astype(x.dtype)

def hybrid_mixer(h, w_in, b_forget, conv_rnn_w, conv_rnn_b, w_rg_a, b_rg_a, w_rg_x, b_rg_x,
                 rg_lambda, norm_attn_out, norm_rnn_out, w_out):
    B, S, _ = h.shape
    proj = h @ w_in
    q, k, v, f_logit, x_rnn, g_rnn = jnp.split(proj, SPLITS, axis=-1)
    q = q.reshape(B, S, N_ATTN_HEADS, HEAD_DIM)
    k = k.reshape(B, S, N_ATTN_HEADS, HEAD_DIM)
    v = v.reshape(B, S, N_ATTN_HEADS, HEAD_DIM)
    log_f = jax.nn.log_sigmoid((f_logit + b_forget).astype(jnp.float32))
    y_attn = forgetting_attention(q, k, v, log_f).reshape(B, S, D_ATTN)
    x_rnn = causal_dwconv(x_rnn, conv_rnn_w, conv_rnn_b)
    y_rnn = rg_lru(x_rnn, w_rg_a, b_rg_a, w_rg_x, b_rg_x, rg_lambda) * jax.nn.gelu(g_rnn)
    y = jnp.concatenate([rmsnorm(y_attn, norm_attn_out), rmsnorm(y_rnn, norm_rnn_out)], axis=-1)
    return y @ w_out

def conv_gated_mlp(h, w_gate, w_up, conv_ffn_w, conv_ffn_b, w_down):
    g = causal_dwconv(h @ w_gate, conv_ffn_w, conv_ffn_b)
    return (jax.nn.gelu(g) * (h @ w_up)) @ w_down

def setup_inputs(seed: int = 0) -> dict:
    key = jax.random.key(seed)
    ks = jax.random.split(key, 24)
    f32 = jnp.float32
    nrm = lambda k, shape, s: jax.random.normal(k, shape, f32) * s
    gain = lambda k, shape: 1.0 + 0.02 * jax.random.normal(k, shape, f32)
    L = DEPTH
    u = jax.random.uniform(ks[10], (L, D_RNN), f32, 0.9, 0.999)
    a0 = u ** (1.0 / RG_C)
    rg_lambda = jnp.log(a0) - jnp.log1p(-a0)
    return {
        "x": jax.random.normal(ks[0], (BATCH, SEQ, D_MODEL), f32),
        "norm_mix_pre": gain(ks[1], (L, D_MODEL)),
        "w_in": nrm(ks[2], (L, D_MODEL, D_IN), D_MODEL ** -0.5),
        "b_forget": 2.0 + 0.5 * jax.random.normal(ks[3], (L, N_ATTN_HEADS), f32),
        "conv_rnn_w": nrm(ks[4], (L, RNN_CONV_W, D_RNN), RNN_CONV_W ** -0.5),
        "conv_rnn_b": nrm(ks[5], (L, D_RNN), 0.01),
        "w_rg_a": nrm(ks[6], (L, N_RNN_BLOCKS, RNN_BLOCK, RNN_BLOCK), RNN_BLOCK ** -0.5),
        "b_rg_a": nrm(ks[7], (L, D_RNN), 0.01),
        "w_rg_x": nrm(ks[8], (L, N_RNN_BLOCKS, RNN_BLOCK, RNN_BLOCK), RNN_BLOCK ** -0.5),
        "b_rg_x": nrm(ks[9], (L, D_RNN), 0.01),
        "rg_lambda": rg_lambda,
        "norm_attn_out": gain(ks[11], (L, D_ATTN)),
        "norm_rnn_out": gain(ks[12], (L, D_RNN)),
        "w_out": nrm(ks[13], (L, D_MIX, D_MODEL), D_MIX ** -0.5),
        "norm_mix_post": gain(ks[14], (L, D_MODEL)),
        "norm_ffn_pre": gain(ks[15], (L, D_MODEL)),
        "w_gate": nrm(ks[16], (L, D_MODEL, D_FF), D_MODEL ** -0.5),
        "w_up": nrm(ks[17], (L, D_MODEL, D_FF), D_MODEL ** -0.5),
        "conv_ffn_w": nrm(ks[18], (L, FFN_CONV_W, D_FF), FFN_CONV_W ** -0.5),
        "conv_ffn_b": nrm(ks[19], (L, D_FF), 0.01),
        "w_down": nrm(ks[20], (L, D_FF, D_MODEL), D_FF ** -0.5),
        "norm_ffn_post": gain(ks[21], (L, D_MODEL)),
    }

def reference(x, norm_mix_pre, w_in, b_forget, conv_rnn_w, conv_rnn_b, w_rg_a, b_rg_a, w_rg_x,
              b_rg_x, rg_lambda, norm_attn_out, norm_rnn_out, w_out, norm_mix_post, norm_ffn_pre,
              w_gate, w_up, conv_ffn_w, conv_ffn_b, w_down, norm_ffn_post):
    for l in range(DEPTH):
        h = rmsnorm(x, norm_mix_pre[l])
        y = hybrid_mixer(h, w_in[l], b_forget[l], conv_rnn_w[l], conv_rnn_b[l], w_rg_a[l], b_rg_a[l],
                         w_rg_x[l], b_rg_x[l], rg_lambda[l], norm_attn_out[l], norm_rnn_out[l], w_out[l])
        x = x + rmsnorm(y, norm_mix_post[l])
        h = rmsnorm(x, norm_ffn_pre[l])
        y = conv_gated_mlp(h, w_gate[l], w_up[l], conv_ffn_w[l], conv_ffn_b[l], w_down[l])
        x = x + rmsnorm(y, norm_ffn_post[l])
    return x


_drawn_inputs = setup_inputs


def setup_inputs(seed=0):
    import zlib

    import numpy as np

    out = dict(_drawn_inputs(seed))
    spreads = {}
    factors = {'b_rg_a': 26.838,
     'b_rg_x': 8.0,
     'norm_attn_out': 16.333,
     'norm_rnn_out': 17.232,
     'norm_mix_post': 3.389,
     'norm_ffn_pre': 3.309,
     'conv_ffn_b': 22.862,
     'norm_ffn_post': 16.402}
    for name, (base, spread) in spreads.items():
        noise = np.random.default_rng([zlib.crc32(name.encode()), seed]).standard_normal(out[name].shape)
        drawn = base * np.exp(spread * noise) if base else spread * noise
        out[name] = __import__('jax').numpy.asarray(drawn.astype(out[name].dtype))
    for name, factor in factors.items():
        out[name] = (out[name] * factor).astype(out[name].dtype)
    return out
```

```python
from contextlib import ExitStack

import concourse.bass as bass
from concourse import mybir

F32 = mybir.dt.float32
F32R = mybir.dt.float32r
ALU = mybir.AluOpType
ACT = mybir.ActivationFunctionType
AXX = mybir.AxisListType.X

P = 128
S = 512
D = 2048
KT = D // P
DA = 1024
NP = DA // P
HD = 64
RG_C = 8.0
FF = 3 * D
FT = FF // P
QT = S // P
UK = 8
UW = UK * P
EPS = 1e-6
SCALE = HD ** -0.5
NEG = -1e30

PER_PAIR = 10
U_MIX = 2
U_OUT = U_MIX + PER_PAIR * NP
U_FF = U_OUT + 2 * KT
U_DOWN = U_FF + 4 * FT
GROUPS = 4
PER_GROUP = FT // 2
NU = U_DOWN + GROUPS * PER_GROUP

COLS = {}
_n = 0
for _name, _w in (("g_pre", KT), ("conv_w", 4 * NP), ("conv_b", NP), ("b_a", NP), ("b_x", NP), ("lam", NP),
                  ("g_y", KT), ("g_post", KT), ("g_ffn", KT), ("ffn_w", 3 * FT), ("ffn_b", FT),
                  ("g_ffn_post", KT), ("b_forget", 1)):
    COLS[_name] = _n
    _n += _w
NPAR = _n

S_SEGS = [(3, 0, 0, 0), (2, 1, 0, 512), (0, 1, 384, 896), (1, 2, 0, 1024)]
S_COL = {q: c for q, _, _, c in S_SEGS}
T_SEGS = [(0, 0, 0, 0), (1, 1, 0, 512), (3, 1, 384, 896), (2, 2, 0, 1024)]
T_COL = {j: c for j, _, _, c in T_SEGS}
T_BANKS = [(0, 512), (512, 512), (1024, 256)]
CAUSAL = 1280
LOG1P = [1.0 / n for n in (15, 13, 11, 9, 7, 5, 3)]


def word(t):
    return t.bitcast(F32)


def at_least(eng, sem, value):
    if isinstance(value, int) and value <= 0:
        return
    eng.wait_ge(sem, value)


class Chain:

    def __init__(self, eng, sem):
        self.eng, self.sem, self.base, self.n = eng, sem, 0, 0

    def __call__(self, instruction):
        self.n += 1
        instruction.then_inc(self.sem, 1)
        self.eng.wait_ge(self.sem, self.base + self.n)

    def loop(self, i, links):
        self.start, self.links = self.base + self.n, links
        self.base, self.n = self.start + i * links, 0

    def end_loop(self, rounds):
        assert self.n == self.links, self.n
        self.base, self.n = self.start + rounds * self.links, 0


def block_kernel(nc, xT, par_d, weights, gate_w, out):
    negc_d = nc.dram_tensor("negc", [2 * NP, S], F32, kind="Internal").ap()
    x1_d = nc.dram_tensor("x1_spill", [P, KT, S], F32, kind="Internal").ap()

    with ExitStack() as ctx:
        def sb_in(stack, name, shape, dt=F32):
            return stack.enter_context(nc.sbuf_tensor(name, [P, *shape], dt))

        def sb(name, shape, dt=F32):
            return sb_in(ctx, name, shape, dt)

        def sem(name):
            return ctx.enter_context(nc.semaphore(name))

        par = sb("par", [NPAR])
        raw = sb("raw", [2, UW])
        w_hi = sb("w_hi", [2, UW], F32R)
        w_lo = sb("w_lo", [2, UW], F32R)
        ones = sb("ones", [P])
        eps = sb("eps", [1])
        rms = sb("rms", [S])
        sq = sb("sq", [2, S])
        std = sq[:, 1]
        acc = sb("acc", [S])
        banks = [ctx.enter_context(nc.psum_tensor(f"bank{i}", [P, S], F32)) for i in range(8)]
        PJ, SB, PT = banks[0:2], banks[2:5], banks[5:8]
        DOWN_BANKS = (banks[4:8], banks[0:4])

        region_a = ExitStack()
        act_hi = sb_in(region_a, "act_hi", [KT, S], F32R)
        act_lo = sb_in(region_a, "act_lo", [KT, S], F32R)
        region_a.close()
        x1_back = sb("x1_back", [KT, S])
        yd = sb("yd", [KT - 4, S])
        h_hi = sb("h_hi", [2, 2 * S], F32R)
        mix = ExitStack()
        y_t = sb_in(mix, "y_t", [KT, S])
        v_t = sb_in(mix, "v_t", [S])
        xr = sb_in(mix, "xr", [S + 4])
        xc = sb_in(mix, "xc", [S])
        xc_hi = sb_in(mix, "xc_hi", [S], F32R)
        xc_lo = sb_in(mix, "xc_lo", [S], F32R)
        gel = sb_in(mix, "gel", [S])
        rg = sb_in(mix, "rg", [S])
        ig = sb_in(mix, "ig", [S])
        tt = sb_in(mix, "tt", [S])
        ae = sb_in(mix, "ae", [S])
        w1 = sb_in(mix, "w1", [S])
        w2 = sb_in(mix, "w2", [S])
        st = sb_in(mix, "st", [S])
        ev = sb_in(mix, "ev", [S])
        q_hi = sb_in(mix, "q_hi", [S], F32R)
        q_lo = sb_in(mix, "q_lo", [S], F32R)
        k_hi = sb_in(mix, "k_hi", [S], F32R)
        k_lo = sb_in(mix, "k_lo", [S], F32R)
        v_hi = sb_in(mix, "v_hi", [QT, P], F32R)
        v_lo = sb_in(mix, "v_lo", [QT, P], F32R)
        pt_hi = [sb_in(mix, f"pt_hi{e}", [CAUSAL], F32R) for e in range(2)]
        pt_lo = [sb_in(mix, f"pt_lo{e}", [CAUSAL], F32R) for e in range(2)]
        sm = sb_in(mix, "sm", [CAUSAL])
        negc = sb_in(mix, "negc_sb", [2, S])
        gw = sb_in(mix, "gw", [2, P])
        gw_hi = sb_in(mix, "gw_hi", [2, P], F32R)
        gw_lo = sb_in(mix, "gw_lo", [2, P], F32R)
        stats = sb_in(mix, "stats", [3, QT])
        lam4 = sb_in(mix, "lam4", [NP])
        lam8 = sb_in(mix, "lam8", [NP])
        lt = sb_in(mix, "lt", [6, NP])
        ident = sb_in(mix, "ident", [P])
        mask = sb_in(mix, "mask", [P])
        acc_b = sb_in(mix, "acc_b", [S])
        mix.close()
        start = ExitStack()
        x_sb = sb_in(start, "x_sb", [KT, S])
        start.close()
        outp = ExitStack()
        sb_in(outp, "y_t_place", [KT, S])
        x1 = sb_in(outp, "x1", [KT, S])
        og = sb_in(outp, "og", [KT, S])
        rms_a = sb_in(outp, "rms_a", [S])
        rms_b = sb_in(outp, "rms_b", [S])
        o1 = sb_in(outp, "o1", [S])
        o2 = sb_in(outp, "o2", [S])
        outp.close()
        ffn = ExitStack()
        h_t = sb_in(ffn, "h_t", [FT, S])
        scratch = ExitStack()
        gb = sb_in(scratch, "gb", [S + 2])
        cv = sb_in(scratch, "cv", [S])
        ge = sb_in(scratch, "ge", [S])
        ub = sb_in(scratch, "ub", [S])
        scratch.close()
        h_lo = sb_in(ffn, "h_lo", [2, 2 * S], F32R)
        ffn.close()
        tail = ExitStack()
        yd_last = sb_in(tail, "yd_last", [4, S])
        tail.close()

        names = """par_landed hi_done split_done unit_used consts_set zeros_set
            act_hi_done act_split sq_done sq_added sum_done std_done rms_set
            f_taken f_negabs f_exp negc_ready negc_stored negc_landed lam_negabs lam_exp lam_ready
            gw_landed gw_hi_done gw_split q_taken q_hi_done q_split k_taken k_hi_done k_split
            v_taken vt_done v_hi_done v_split x_taken xc_done xc_hi_done xc_split g_taken gel_done
            qk_done s_taken max_done exp_done probs_ready pt_done pt_hi_done pt_split pv_done ya_taken
            gates_done gates_taken gate_funcs yr_done ysq_done ynorm_ready wo_taken o_done osq_done osum_ready
            res_landed og_scaled x1_done x1_stored x1_landed x1sq_done x1sq_used
            gate_taken conv_done gelu_done up_taken h_done h_hi_done h_split
            wd_taken wdsq_done wdsum_ready yd_scaled out_ready stored dve_chain""".split()
        (par_landed, hi_done, split_done, unit_used, consts_set, zeros_set,
         act_hi_done, act_split, sq_done, sq_added, sum_done, std_done, rms_set,
         f_taken, f_negabs, f_exp, negc_ready, negc_stored, negc_landed, lam_negabs, lam_exp, lam_ready,
         gw_landed, gw_hi_done, gw_split, q_taken, q_hi_done, q_split, k_taken, k_hi_done, k_split,
         v_taken, vt_done, v_hi_done, v_split, x_taken, xc_done, xc_hi_done, xc_split, g_taken, gel_done,
         qk_done, s_taken, max_done, exp_done, probs_ready, pt_done, pt_hi_done, pt_split, pv_done, ya_taken,
         gates_done, gates_taken, gate_funcs, yr_done, ysq_done, ynorm_ready, wo_taken, o_done, osq_done, osum_ready,
         res_landed, og_scaled, x1_done, x1_stored, x1_landed, x1sq_done, x1sq_used,
         gate_taken, conv_done, gelu_done, up_taken, h_done, h_hi_done, h_split,
         wd_taken, wdsq_done, wdsum_ready, yd_scaled, out_ready, stored, dve_chain) = [sem(n) for n in names]
        x_landed = [sem(f"x_landed{c}") for c in range(4)]
        raw_landed = [sem(f"raw_landed{s}") for s in range(2)]

        def col(name, i=0):
            c = COLS[name] + i
            return par[:, c:c + 1] if isinstance(c, int) else par[:, bass.ds(c, 1)]

        def tile_of(t, i, part=slice(0, P)):
            return t[part, i] if isinstance(i, int) else t[part, bass.ds(i, 1), :].rearrange("p a s -> p (a s)")

        def two_tiles(t, ku):
            return t[:, bass.ds(ku * 2, 2), :].rearrange("p a s -> p (a s)")

        def one_col(t, i):
            return t[:, i:i + 1] if isinstance(i, int) else t[:, bass.ds(i, 1)]

        def flat(t):
            return t[:].rearrange("p a s -> p (a s)")

        def yd_tile(k):
            return yd[:, k] if k < KT - 4 else yd_last[:, k - (KT - 4)]

        block = ctx.enter_context(nc.Block())

        @block.sync
        def _(sp):
            sp.dma_start(par[:], par_d).then_inc(par_landed, 16)
            for c in range(4):
                sp.dma_start(x_sb[:, 4 * c:4 * c + 4], xT[:, 4 * c:4 * c + 4]).then_inc(x_landed[c], 16)
                if c < 2:
                    sp.dma_start(raw[:, c], weights[c]).then_inc(raw_landed[c], 16)
            with sp.Fori(1, NU // 2) as t:
                for s in range(2):
                    sp.wait_ge(split_done, t * 2 + (s - 1))
                    sp.dma_start(raw[:, s], weights[bass.ds(t * 2 + s, 1)].rearrange("a p n -> p (a n)")).then_inc(
                        raw_landed[s], 16)
            for c in range(4):
                sp.wait_ge(out_ready, 4 * (c + 1))
                sp.dma_start(out[:, 4 * c:4 * c + 4], x1_back[:, 4 * c:4 * c + 4]).then_inc(stored, 16)
            sp.wait_ge(stored, 64)

        @block.gpsimd
        def _(pool):
            pool.dma_start(gw[:], gate_w[0]).then_inc(gw_landed, 16)
            pool.memset(eps[:], EPS)
            pool.memset(ones[:], 1.0).then_inc(consts_set, 1)
            pool.memset(ident[:], 0.0).then_inc(zeros_set, 1)
            pool.memset(mask[:], 0.0).then_inc(zeros_set, 1)
            pool.memset(xr[:, 0:4], 0.0).then_inc(zeros_set, 1)
            pool.memset(acc[:], 0.0).then_inc(zeros_set, 1)
            pool.wait_ge(zeros_set, 4)
            pool.affine_select(out=ident[:], in_=ident[:], compare_op=ALU.not_equal, fill=1.0, base=0,
                               pattern=[[-1, P]], channel_multiplier=1).then_inc(consts_set, 1)
            pool.affine_select(out=mask[:], in_=mask[:], compare_op=ALU.is_ge, fill=NEG, base=0,
                               pattern=[[-1, P]], channel_multiplier=1).then_inc(consts_set, 1)
            for k in range(KT):
                pool.wait_ge(sq_done, k + 1)
                if k:
                    pool.wait_ge(sq_added, k)
                pool.tensor_tensor(acc[:], acc[:], sq[:, k % 2], ALU.add).then_inc(sq_added, 1)
            pool.wait_ge(negc_ready, 1)
            pool.dma_start(negc_d, tt[0:2 * NP]).then_inc(negc_stored, 16)
            pool.wait_ge(negc_stored, 16)
            pool.dma_start(negc[:], negc_d[0:2].partition_broadcast(P)).then_inc(negc_landed, 16)
            with pool.Fori(1, NP) as p:
                pool.wait_ge(gw_split, p)
                pool.dma_start(gw[:], gate_w[bass.ds(p, 1)].rearrange("a p m n -> p (a m) n")).then_inc(gw_landed, 16)
                pool.wait_ge(s_taken, p * 6)
                pool.dma_start(negc[:], negc_d[bass.ds(p * 2, 2)].partition_broadcast(P)).then_inc(negc_landed, 16)
            pool.wait_ge(yr_done, NP)
            pool.wait_ge(act_split, 2 * KT)
            pool.dma_start(x1[:], xT).then_inc(res_landed, 16)
            pool.wait_ge(rms_set, 4)
            with pool.Fori(0, KT) as k:
                pool.tensor_tensor(tile_of(og, k), tile_of(og, k), rms[:], ALU.mult).then_inc(og_scaled, 1)
            pool.wait_ge(x1_done, KT)
            pool.dma_start(x1_d, x1[:]).then_inc(x1_stored, 16)
            pool.wait_ge(x1_stored, 16)
            pool.wait_ge(unit_used, U_DOWN)
            pool.dma_start(x1_back[:], x1_d).then_inc(x1_landed, 16)
            pool.wait_ge(x1_landed, 16)
            pool.wait_ge(wdsum_ready, 1)
            pool.wait_ge(rms_set, 6)
            for k in range(KT // 2, KT):
                pool.tensor_tensor(yd_tile(k), yd_tile(k), rms[:], ALU.mult).then_inc(yd_scaled, 1)

        @block.scalar
        def _(act):
            def split(u, s):
                act.wait_ge(raw_landed[s], (u - s) * 8 + 16)
                at_least(act, unit_used, u - 1)
                act.activation(w_hi[:, s], raw[:, s], ACT.Copy).then_inc(hi_done, 1)

            def split_h(n, s, ku):
                act.wait_ge(unit_used, n + (U_DOWN - 1))
                act.activation(h_hi[:, s], two_tiles(h_t, ku), ACT.Copy).then_inc(h_hi_done, 1)

            def root(n, bank, width=D):
                act.wait_ge(sum_done, n)
                at_least(act, rms_set, n - 1)
                act.activation(std, bank[:], ACT.Sqrt, scale=1.0 / width, bias=eps[:, 0:1]).then_inc(std_done, 1)

            def pt_his(n, e):
                for b, (c, w) in enumerate(T_BANKS):
                    act.wait_ge(pt_done, n * 3 + (b + 1))
                    act.activation(pt_hi[e][:, c:c + w], PT[b][:, 0:w], ACT.Copy).then_inc(pt_hi_done, 1)

            def exps(n):
                for i, (qt, _, _, c) in enumerate(S_SEGS):
                    act.wait_ge(max_done, n * 4 + (i + 1))
                    seg = sm[:, c:c + P * (qt + 1)]
                    act.activation(seg, seg, ACT.Exp, bias=stats[:, 0, i:i + 1],
                                   accum_out=stats[:, 1, i:i + 1]).then_inc(exp_done, 1)

            def gates(p):
                act.wait_ge(gates_done, p)
                act.activation(rg[:], SB[1][:], ACT.Sigmoid, bias=col("b_a", p - 1)).then_inc(gates_taken, 1)
                act.activation(ig[:], SB[2][:], ACT.Sigmoid, bias=col("b_x", p - 1)).then_inc(gates_taken, 1)

            def gate_functions(p):
                act.wait_ge(gates_taken, p * 2)
                act.activation(tt[:], rg[:], ACT.Tanh, scale=one_col(lam4, p - 1)).then_inc(gate_funcs, 1)
                act.activation(ae[:], rg[:], ACT.Exp, scale=one_col(lam8, p - 1)).then_inc(gate_funcs, 1)
                act.wait_ge(gate_funcs, p * 3 - 1)
                act.activation(st[:], tt[:], ACT.Sqrt).then_inc(gate_funcs, 1)

            def v_his(p):
                act.wait_ge(vt_done, p)
                act.activation(flat(v_hi), PJ[1][:], ACT.Copy).then_inc(v_hi_done, 1)

            def y_squares(p):
                act.wait_ge(ya_taken, p * 2)
                act.activation(sq[:, 0], tile_of(y_t, p - 1), ACT.Square).then_inc(ysq_done, 1)
                act.wait_ge(yr_done, p)
                act.activation(sq[:, 1], tile_of(y_t, p + (NP - 1)), ACT.Square).then_inc(ysq_done, 1)

            def pair(p, prev):
                u = p * PER_PAIR + U_MIX
                split(u + 1, 1)
                if prev:
                    gates(p)
                    pt_his(p * 2 - 1, 1)
                split(u + 2, 0)
                if prev:
                    v_his(p)
                    gate_functions(p)
                else:
                    root(1, SB[2])
                split(u + 3, 1)
                act.wait_ge(q_taken, p + 1)
                act.activation(q_hi[:], ev[:], ACT.Copy).then_inc(q_hi_done, 1)
                if not prev:
                    act.wait_ge(f_negabs, 1)
                    act.activation(w1[0:2 * NP], w1[0:2 * NP], ACT.Exp).then_inc(f_exp, 1)
                split(u + 4, 0)
                split(u + 5, 1)
                if prev:
                    y_squares(p)
                act.wait_ge(k_taken, p + 1)
                act.activation(k_hi[:], ev[:], ACT.Copy).then_inc(k_hi_done, 1)
                act.wait_ge(gw_landed, p * 16 + 16)
                act.activation(gw_hi[:], gw[:], ACT.Copy).then_inc(gw_hi_done, 1)
                split(u + 6, 0)
                split(u + 7, 1)
                exps(p * 2)
                split(u + 8, 0)
                act.wait_ge(xc_done, p + 1)
                act.activation(xc_hi[:], xc[:], ACT.Copy).then_inc(xc_hi_done, 1)
                split(u + 9, 1)
                pt_his(p * 2, 0)
                exps(p * 2 + 1)
                split(u + 10, 0)
                act.wait_ge(g_taken, p + 1)
                act.activation(gel[:], ev[:], ACT.Gelu_apprx_tanh).then_inc(gel_done, 1)

            act.wait_ge(consts_set, 1)
            act.wait_ge(par_landed, 16)
            split(0, 0)
            for k in range(KT):
                if k % 4 == 0:
                    act.wait_ge(x_landed[k // 4], 16)
                act.activation(act_hi[:, k], x_sb[:, k], ACT.Copy, scale=col("g_pre", k)).then_inc(act_hi_done, 1)
                if k == UK - 1:
                    split(1, 1)
                at_least(act, sq_added, k - 1)
                act.activation(sq[:, k % 2], x_sb[:, k], ACT.Square).then_inc(sq_done, 1)
            act.wait_ge(lam_negabs, 1)
            act.activation(lt[:, 1], lt[:, 0], ACT.Exp).then_inc(lam_exp, 1)
            split(2, 0)
            pair(0, False)
            act.wait_ge(lam_ready, 1)
            with act.Fori(1, NP) as p:
                pair(p, True)

            def y_hi(k):
                act.activation(act_hi[:, k], y_t[:, k], ACT.Copy, scale=col("g_y", k)).then_inc(act_hi_done, 1)

            gates(NP)
            pt_his(2 * NP - 1, 1)
            act.wait_ge(unit_used, U_OUT)
            for k in range(3):
                y_hi(k)
            v_his(NP)
            gate_functions(NP)
            for k in range(3, NP - 1):
                y_hi(k)
            act.wait_ge(ya_taken, 2 * NP)
            y_hi(NP - 1)
            for k in range(NP, KT - 1):
                y_hi(k)
            split(U_OUT + 1, 1)
            act.wait_ge(yr_done, NP)
            y_hi(KT - 1)
            y_squares(NP)
            split(U_OUT + 2, 0)
            root(2, SB[2], DA)
            root(3, PT[2], DA)

            def out_square(t):
                act.wait_ge(o_done, t + 1)
                act.activation(sq[:, 0], o1[:], ACT.Square).then_inc(osq_done, 1)

            split(U_OUT + 3, 1)
            out_square(0)
            split(U_OUT + 4, 0)
            with act.Fori(2, KT) as t:
                split(t * 2 + (U_OUT + 1), 1)
                out_square(t - 1)
                split(t * 2 + (U_OUT + 2), 0)
            out_square(KT - 1)
            split(U_FF + 1, 1)
            root(4, SB[2])

            with act.Fori(0, KT) as k:
                act.wait_ge(x1_done, k + 1)
                act.activation(tile_of(act_hi, k), tile_of(x1, k), ACT.Copy, scale=col("g_ffn", k)).then_inc(
                    act_hi_done, 1)
                act.wait_ge(std_done, 4)
                act.wait_ge(x1sq_used, k + 1)
                act.activation(sq[:, 0], tile_of(x1, k), ACT.Square).then_inc(x1sq_done, 1)

            def gelu_gate(j):
                act.wait_ge(conv_done, j + 1)
                act.activation(ge[:], cv[:], ACT.Gelu_apprx_tanh).then_inc(gelu_done, 1)

            split(U_FF + 2, 0)
            root(5, SB[2])
            split(U_FF + 3, 1)
            gelu_gate(0)
            split(U_FF + 4, 0)
            with act.Fori(1, FT) as j:
                split(j * 4 + (U_FF + 1), 1)
                split(j * 4 + (U_FF + 2), 0)
                split(j * 4 + (U_FF + 3), 1)
                gelu_gate(j)
                split(j * 4 + (U_FF + 4), 0)

            act.wait_ge(unit_used, U_DOWN)
            act.wait_ge(h_done, FT)
            split_h(0, 0, 0)

            def both(n, s, ku):
                split(n + U_DOWN, s)
                split_h(n, s, ku)

            def down_squares(g):
                for i in range(4):
                    act.wait_ge(wd_taken, 4 * g + i + 1)
                    act.activation(sq[:, 0], sq[:, 1], ACT.Square).then_inc(wdsq_done, 1)

            for g in range(GROUPS):
                n = g * PER_GROUP
                both(n + 1, 1, 1)
                if g:
                    down_squares(g - 1)
                both(n + 2, 0, 2)
                with act.Fori(1, PER_GROUP // 2 - 1) as t:
                    both(t * 2 + (n + 1), 1, t * 2 + 1)
                    both(t * 2 + (n + 2), 0, t * 2 + 2)
                both(n + PER_GROUP - 1, 1, PER_GROUP - 1)
                if g < GROUPS - 1:
                    both(n + PER_GROUP, 0, 0)
            down_squares(GROUPS - 1)
            root(6, SB[2])

        @block.vector
        def _(dve):
            chain = Chain(dve, dve_chain)

            def split(u, s):
                dve.wait_ge(hi_done, u + 1)
                dve.tensor_tensor(w_lo[:, s], raw[:, s], word(w_hi[:, s]), ALU.subtract).then_inc(split_done, 1)

            def split_h(n, s, ku):
                dve.wait_ge(h_hi_done, n + 1)
                dve.tensor_tensor(h_lo[:, s], two_tiles(h_t, ku), word(h_hi[:, s]), ALU.subtract).then_inc(h_split, 1)

            def lo_of_scaled(k, src, gain, n):
                dve.wait_ge(act_hi_done, n + 1)
                dve.scalar_tensor_tensor(out=tile_of(act_lo, k), in0=tile_of(src, k), scalar=col(gain, k),
                                         in1=word(tile_of(act_hi, k)), op0=ALU.mult,
                                         op1=ALU.subtract).then_inc(act_split, 1)

            def invert_root(n, dst):
                dve.wait_ge(std_done, n)
                dve.reciprocal(dst, std).then_inc(rms_set, 1)
                dve.wait_ge(rms_set, n)

            def log1p_half(y, s, z, w):
                chain(dve.tensor_scalar(s, y, 2.0, None, ALU.add))
                chain(dve.reciprocal(s, s))
                chain(dve.tensor_tensor(s, y, s, ALU.mult))
                chain(dve.tensor_tensor(z, s, s, ALU.mult))
                chain(dve.tensor_scalar(w, z, LOG1P[0], None, ALU.mult))
                for c in LOG1P[1:]:
                    chain(dve.scalar_tensor_tensor(out=w, in0=w, scalar=c, in1=z, op0=ALU.add, op1=ALU.mult))
                chain(dve.scalar_tensor_tensor(out=w, in0=w, scalar=1.0, in1=s, op0=ALU.add, op1=ALU.mult))

            lam = par[:, COLS["lam"]:COLS["lam"] + NP]

            def lambda_terms():
                chain(dve.tensor_scalar(lt[:, 5], lam, -1.0, 0.0, ALU.mult, ALU.max))
                dve.wait_ge(lam_exp, 1)
                log1p_half(lt[:, 1], lt[:, 2], lt[:, 3], lt[:, 4])
                chain(dve.scalar_tensor_tensor(out=lt[:, 4], in0=lt[:, 4], scalar=2.0, in1=lt[:, 5], op0=ALU.mult,
                                               op1=ALU.add))
                dve.tensor_scalar(lam4[:], lt[:, 4], RG_C / 2, None, ALU.mult)
                dve.tensor_scalar(lam8[:], lt[:, 4], -RG_C, None, ALU.mult).then_inc(lam_ready, 1)

            H = 2 * NP

            def forget_logits():
                dve.tensor_tensor(v_t[0:H], PJ[0][0:H], rms[0:H], ALU.mult).then_inc(f_taken, 1)
                dve.wait_ge(f_taken, 1)
                chain(dve.tensor_scalar(v_t[0:H], v_t[0:H], par[0:H, COLS["b_forget"]:COLS["b_forget"] + 1], None,
                                        ALU.add))
                dve.scalar_tensor_tensor(out=w1[0:H], in0=v_t[0:H], scalar=-1.0, in1=v_t[0:H], op0=ALU.mult,
                                         op1=ALU.min).then_inc(f_negabs, 1)

            def forget_sums():
                dve.wait_ge(f_exp, 1)
                chain(dve.memset(st[0:H], 1.0))
                log1p_half(w1[0:H], w2[0:H], rg[0:H], ig[0:H])
                chain(dve.tensor_scalar(v_t[0:H], v_t[0:H], 0.0, None, ALU.min))
                chain(dve.scalar_tensor_tensor(out=v_t[0:H], in0=ig[0:H], scalar=-2.0, in1=v_t[0:H], op0=ALU.mult,
                                               op1=ALU.add))
                dve.tensor_tensor_scan(tt[0:H], st[0:H], v_t[0:H], 0.0, ALU.mult, ALU.subtract).then_inc(
                    negc_ready, 1)

            def pt_los(n, e):
                for b, (c, w) in enumerate(T_BANKS):
                    dve.wait_ge(pt_hi_done, n * 3 + (b + 1))
                    dve.tensor_tensor(pt_lo[e][:, c:c + w], PT[b][:, 0:w], word(pt_hi[e][:, c:c + w]),
                                      ALU.subtract).then_inc(pt_split, 1)

            def logits(n, e, p):
                if e == 0:
                    dve.wait_ge(negc_landed, p * 16 + 16)
                for i, (qt, b, bc, c) in enumerate(S_SEGS):
                    w = P * (qt + 1)
                    dve.wait_ge(qk_done, n * 3 + (b + 1))
                    ins = dve.scalar_tensor_tensor(out=sm[:, c:c + w], in0=SB[b][:, bc:bc + w], scalar=SCALE,
                                                   in1=negc[:, e, 0:w], op0=ALU.mult, op1=ALU.add)
                    if i == 1:
                        chain(ins)
                    else:
                        ins.then_inc(s_taken, 1)
                        dve.wait_ge(s_taken, n * 3 + (b + 1))
                    diag = sm[:, c + w - P:c + w]
                    chain(dve.tensor_tensor(diag, diag, mask[:], ALU.add))
                    dve.tensor_reduce(stats[:, 0, i:i + 1], sm[:, c:c + w], AXX, ALU.max, negate=True).then_inc(
                        max_done, 1)

            def probabilities(n):
                dve.wait_ge(exp_done, n * 4 + 4)
                chain(dve.reciprocal(stats[:, 2], stats[:, 1]))
                for i, (qt, _, _, c) in enumerate(S_SEGS):
                    seg = sm[:, c:c + P * (qt + 1)]
                    ins = dve.tensor_scalar(seg, seg, stats[:, 2, i:i + 1], None, ALU.mult)
                ins.then_inc(probs_ready, 1)

            def v_out(p):
                dve.wait_ge(unit_used, p * PER_PAIR + U_MIX)
                dve.tensor_tensor(v_t[:], PJ[0][:], rms[:], ALU.mult).then_inc(v_taken, 1)

            def v_los(p):
                dve.wait_ge(v_hi_done, p)
                dve.tensor_tensor(flat(v_lo), PJ[1][:], word(flat(v_hi)), ALU.subtract).then_inc(v_split, 1)

            def decay(p):
                dve.wait_ge(gate_funcs, p * 3 - 1)
                chain(dve.scalar_tensor_tensor(out=w1[:], in0=ae[:], scalar=1.0, in1=tt[:], op0=ALU.add,
                                               op1=ALU.mult))
                chain(dve.tensor_scalar(w2[:], w1[:], -1.0, 1.0, ALU.mult, ALU.add))
                chain(dve.scalar_tensor_tensor(out=ae[:], in0=tt[:], scalar=0.5, in1=ae[:], op0=ALU.is_ge,
                                               op1=ALU.mult))
                chain(dve.scalar_tensor_tensor(out=w2[:], in0=tt[:], scalar=0.5, in1=w2[:], op0=ALU.is_lt,
                                               op1=ALU.mult))
                chain(dve.tensor_tensor(ae[:], ae[:], w2[:], ALU.add))

            def recurrence(p):
                dve.wait_ge(gate_funcs, p * 3)
                chain(dve.scalar_tensor_tensor(out=w2[:], in0=ae[:], scalar=1.0, in1=st[:], op0=ALU.add,
                                               op1=ALU.mult))
                chain(dve.memset(w2[:, 0:1], 1.0))
                chain(dve.tensor_tensor(w2[:], w2[:], ig[:], ALU.mult))
                chain(dve.tensor_tensor(w1[:], w2[:], xc[:], ALU.mult))
                chain(dve.tensor_tensor_scan(w2[:], ae[:], w1[:], 0.0, ALU.mult, ALU.add))
                dve.wait_ge(gel_done, p)
                dve.tensor_tensor(tile_of(y_t, p + (NP - 1)), w2[:], gel[:], ALU.mult).then_inc(yr_done, 1)

            def attention_out(p):
                for e in range(2):
                    dve.wait_ge(pv_done, p * 2 - 1 + e)
                    h = slice(HD * e, HD * e + HD)
                    dve.tensor_copy(tile_of(y_t, p - 1, h), PJ[e][h, :]).then_inc(ya_taken, 1)

            def add_squares(p, last=False):
                for e, a in enumerate((acc, acc_b)):
                    dve.wait_ge(ysq_done, p * 2 - 1 + e)
                    ins = dve.tensor_tensor(a[:], a[:], sq[:, e], ALU.add)
                    ins.then_inc(ynorm_ready, 1) if last else chain(ins)

            def pair(p, prev):
                u = p * PER_PAIR + U_MIX
                split(u + 1, 1)
                if prev:
                    v_out(p)
                    pt_los(p * 2 - 1, 1)
                split(u + 2, 0)
                if prev:
                    v_los(p)
                    decay(p)
                else:
                    lambda_terms()
                    invert_root(1, rms[:])
                    chain(dve.memset(acc[:], 0.0))
                    chain(dve.memset(acc_b[:], 0.0))
                split(u + 3, 1)
                dve.wait_ge(unit_used, u + 2)
                dve.tensor_tensor(ev[:], SB[0][:], rms[:], ALU.mult).then_inc(q_taken, 1)
                if prev:
                    attention_out(p)
                dve.wait_ge(q_hi_done, p + 1)
                dve.tensor_tensor(q_lo[:], ev[:], word(q_hi[:]), ALU.subtract).then_inc(q_split, 1)
                if not prev:
                    forget_logits()
                split(u + 4, 0)
                if prev:
                    recurrence(p)
                else:
                    forget_sums()
                split(u + 5, 1)
                dve.wait_ge(unit_used, u + 4)
                dve.tensor_tensor(ev[:], SB[1][:], rms[:], ALU.mult).then_inc(k_taken, 1)
                dve.wait_ge(k_hi_done, p + 1)
                dve.tensor_tensor(k_lo[:], ev[:], word(k_hi[:]), ALU.subtract).then_inc(k_split, 1)
                dve.wait_ge(gw_hi_done, p + 1)
                dve.tensor_tensor(gw_lo[:], gw[:], word(gw_hi[:]), ALU.subtract).then_inc(gw_split, 1)
                if prev:
                    add_squares(p)
                split(u + 6, 0)
                split(u + 7, 1)
                logits(p * 2, 0, p)
                probabilities(p * 2)
                split(u + 8, 0)
                dve.wait_ge(unit_used, u + 6)
                dve.tensor_tensor(xr[:, 4:], PJ[0][:], rms[:], ALU.mult).then_inc(x_taken, 1)
                dve.wait_ge(x_taken, p + 1)
                chain(dve.tensor_scalar(xc[:], xr[:, 4:4 + S], col("conv_w", p + 3 * NP), col("conv_b", p), ALU.mult,
                                        ALU.add))
                for tap in (2, 1, 0):
                    ins = dve.scalar_tensor_tensor(out=xc[:], in0=xr[:, 1 + tap:1 + tap + S],
                                                   scalar=col("conv_w", p + tap * NP), in1=xc[:], op0=ALU.mult,
                                                   op1=ALU.add)
                    chain(ins) if tap else ins.then_inc(xc_done, 1)
                dve.wait_ge(xc_hi_done, p + 1)
                dve.tensor_tensor(xc_lo[:], xc[:], word(xc_hi[:]), ALU.subtract).then_inc(xc_split, 1)
                split(u + 9, 1)
                dve.wait_ge(unit_used, u + 8)
                dve.tensor_tensor(ev[:], PJ[1][:], rms[:], ALU.mult).then_inc(g_taken, 1)
                logits(p * 2 + 1, 1, p)
                pt_los(p * 2, 0)
                split(u + 10, 0)
                probabilities(p * 2 + 1)

            dve.wait_ge(par_landed, 16)
            dve.scalar_tensor_tensor(out=lt[:, 0], in0=lam, scalar=-1.0, in1=lam, op0=ALU.mult,
                                     op1=ALU.min).then_inc(lam_negabs, 1)
            split(0, 0)
            for k in range(KT):
                lo_of_scaled(k, x_sb, "g_pre", k)
                if k == UK - 1:
                    split(1, 1)
            split(2, 0)
            dve.wait_ge(consts_set, 3)
            pair(0, False)
            with dve.Fori(1, NP) as p:
                chain.loop(p - 1, 5 + 5 + 2 + 5 + 1 + 3 + 5 + 1)
                pair(p, True)
                chain.end_loop(NP - 1)

            v_out(NP)
            pt_los(2 * NP - 1, 1)
            for k in range(3):
                lo_of_scaled(k, y_t, "g_y", KT + k)
            v_los(NP)
            for k in range(3, NP - 1):
                lo_of_scaled(k, y_t, "g_y", KT + k)
            decay(NP)
            attention_out(NP)
            lo_of_scaled(NP - 1, y_t, "g_y", KT + NP - 1)
            recurrence(NP)
            for k in range(NP, KT - 1):
                lo_of_scaled(k, y_t, "g_y", KT + k)
            split(U_OUT + 1, 1)
            lo_of_scaled(KT - 1, y_t, "g_y", 2 * KT - 1)
            add_squares(NP, True)
            split(U_OUT + 2, 0)
            invert_root(2, rms_a[:])
            invert_root(3, rms_b[:])
            chain(dve.memset(acc[:], 0.0))
            split(U_OUT + 3, 1)

            def out_tile(t, s):
                first, second = ((SB[0], SB[1]), (PT[0], PT[1]))[s]
                dve.wait_ge(unit_used, t * 2 + (U_OUT + 2))
                chain(dve.tensor_tensor(o1[:], first[:], rms_a[:], ALU.mult))
                dve.tensor_tensor(o2[:], second[:], rms_b[:], ALU.mult).then_inc(wo_taken, 1)
                dve.wait_ge(wo_taken, t + 1)
                dve.tensor_tensor(o1[:], o1[:], o2[:], ALU.add).then_inc(o_done, 1)
                dve.wait_ge(o_done, t + 1)
                dve.tensor_scalar(tile_of(og, t), o1[:], col("g_post", t), None, ALU.mult)
                dve.wait_ge(osq_done, t + 1)
                ins = dve.tensor_tensor(acc[:], acc[:], sq[:, 0], ALU.add)
                ins.then_inc(osum_ready, 1) if isinstance(t, int) and t == KT - 1 else chain(ins)

            out_tile(0, 0)
            split(U_OUT + 4, 0)
            with dve.Fori(1, KT // 2) as i:
                chain.loop(i - 1, 4)
                split(i * 4 + (U_OUT + 1), 1)
                out_tile(i * 2 - 1, 1)
                split(i * 4 + (U_OUT + 2), 0)
                split(i * 4 + (U_OUT + 3), 1)
                out_tile(i * 2, 0)
                split(i * 4 + (U_OUT + 4), 0)
                chain.end_loop(KT // 2 - 1)
            out_tile(KT - 1, 1)
            split(U_FF + 1, 1)
            invert_root(4, rms[:])
            dve.wait_ge(res_landed, 16)
            with dve.Fori(0, KT) as k:
                dve.wait_ge(og_scaled, k + 1)
                dve.tensor_tensor(tile_of(x1, k), tile_of(x1, k), tile_of(og, k), ALU.add).then_inc(x1_done, 1)
                dve.wait_ge(x1_done, k + 1)
                lo_of_scaled(k, x1, "g_ffn", k + 2 * KT)

            def gate_tile(j):
                dve.wait_ge(unit_used, j * 4 + (U_FF + 2))
                dve.tensor_tensor(gb[:, 2:], PJ[0][:], rms[:], ALU.mult).then_inc(gate_taken, 1)
                dve.wait_ge(gate_taken, j + 1)
                chain(dve.tensor_scalar(cv[:], gb[:, 2:2 + S], col("ffn_w", j + 2 * FT), col("ffn_b", j), ALU.mult,
                                        ALU.add))
                chain(dve.scalar_tensor_tensor(out=cv[:], in0=gb[:, 1:1 + S], scalar=col("ffn_w", j + FT), in1=cv[:],
                                               op0=ALU.mult, op1=ALU.add))
                dve.scalar_tensor_tensor(out=cv[:], in0=gb[:, 0:S], scalar=col("ffn_w", j), in1=cv[:],
                                         op0=ALU.mult, op1=ALU.add).then_inc(conv_done, 1)

            def up_tile(j):
                dve.wait_ge(unit_used, j * 4 + (U_FF + 4))
                dve.tensor_tensor(ub[:], PJ[1][:], rms[:], ALU.mult).then_inc(up_taken, 1)
                dve.wait_ge(up_taken, j + 1)
                dve.wait_ge(gelu_done, j + 1)
                dve.tensor_tensor(tile_of(h_t, j), ub[:], ge[:], ALU.mult).then_inc(h_done, 1)

            split(U_FF + 2, 0)
            invert_root(5, rms[:])
            chain(dve.memset(gb[:, 0:2], 0.0))
            chain(dve.memset(acc[:], 0.0))
            split(U_FF + 3, 1)
            gate_tile(0)
            split(U_FF + 4, 0)
            dve.wait_ge(x1_stored, 16)
            with dve.Fori(1, FT) as j:
                chain.loop(j - 1, 2)
                split(j * 4 + (U_FF + 1), 1)
                up_tile(j - 1)
                split(j * 4 + (U_FF + 2), 0)
                split(j * 4 + (U_FF + 3), 1)
                gate_tile(j)
                split(j * 4 + (U_FF + 4), 0)
                chain.end_loop(FT - 1)
            up_tile(FT - 1)
            split_h(0, 0, 0)

            def both(n, s, ku):
                split(n + U_DOWN, s)
                split_h(n, s, ku)

            def down_tiles(g):
                for i in range(4):
                    t = 4 * g + i
                    if i == 0:
                        dve.wait_ge(unit_used, U_DOWN + (g + 1) * PER_GROUP)
                    dve.tensor_copy(sq[:, 1], DOWN_BANKS[g % 2][i][:]).then_inc(wd_taken, 1)
                    dve.wait_ge(wd_taken, t + 1)
                    dve.tensor_scalar(yd_tile(t), sq[:, 1], col("g_ffn_post", t), None, ALU.mult)
                    dve.wait_ge(wdsq_done, t + 1)
                    ins = dve.tensor_tensor(acc[:], acc[:], sq[:, 0], ALU.add)
                    ins.then_inc(wdsum_ready, 1) if t == KT - 1 else chain(ins)

            for g in range(GROUPS):
                n = g * PER_GROUP
                both(n + 1, 1, 1)
                if g:
                    down_tiles(g - 1)
                both(n + 2, 0, 2)
                with dve.Fori(1, PER_GROUP // 2 - 1) as t:
                    both(t * 2 + (n + 1), 1, t * 2 + 1)
                    both(t * 2 + (n + 2), 0, t * 2 + 2)
                both(n + PER_GROUP - 1, 1, PER_GROUP - 1)
                if g < GROUPS - 1:
                    both(n + PER_GROUP, 0, 0)
            down_tiles(GROUPS - 1)
            invert_root(6, rms[:])
            dve.wait_ge(x1_landed, 16)
            for k in range(KT):
                if k < KT // 2:
                    chain(dve.tensor_tensor(yd_tile(k), yd_tile(k), rms[:], ALU.mult))
                else:
                    dve.wait_ge(yd_scaled, k - KT // 2 + 1)
                dve.tensor_tensor(x1_back[:, k], x1_back[:, k], yd_tile(k), ALU.add).then_inc(out_ready, 1)

        @block.tensor
        def _(pe):
            def product(dst, a, b, start, stop):
                (ah, al), (bh, bl) = a, b
                pe.matmul(dst, ah, bh, start=start, stop=False)
                pe.matmul(dst, ah, bl, start=False, stop=False)
                return pe.matmul(dst, al, bh, start=False, stop=stop)

            def w_tile(s, c):
                return w_hi[:, s, c * P:c * P + P], w_lo[:, s, c * P:c * P + P]

            def unit(u, s, half, bank, start, stop, each=None):
                pe.wait_ge(split_done, u + 1)
                for i in range(UK):
                    k = half * UK + i
                    if each:
                        each(k)
                    last = product(bank[:], w_tile(s, i), (act_hi[:, k], act_lo[:, k]),
                                   start and i == 0, stop and i == UK - 1)
                last.then_inc(unit_used, 1)

            def tile(u, bank, between=None):
                unit(u, 0, 0, bank, True, False)
                if between:
                    between()
                unit(u + 1, 1, 1, bank, False, True)

            def channel_sum(bank, src):
                pe.matmul(bank[:], ones[:], src, start=True, stop=True).then_inc(sum_done, 1)

            def scores(n, e):
                h = slice(HD * e, HD * e + HD)
                for i, (qt, b, bc, _) in enumerate(S_SEGS):
                    q = slice(P * qt, P * qt + P)
                    keys = slice(0, P * (qt + 1))
                    last = product(SB[b][:, bc:bc + P * (qt + 1)], (q_hi[h, q], q_lo[h, q]),
                                   (k_hi[h, keys], k_lo[h, keys]), True, True)
                    if i != 1:
                        last.then_inc(qk_done, 1)

            def transposes(n, e):
                pe.wait_ge(probs_ready, n + 1)
                at_least(pe, pt_split, n * 3)
                for i, (j, b, bc, _) in enumerate(T_SEGS):
                    for qt in range(j, QT):
                        c = S_COL[qt] + P * j
                        last = pe.transpose(PT[b][:, bc + P * (qt - j):bc + P * (qt - j) + P], sm[:, c:c + P],
                                            ident[:])
                    if i != 1:
                        last.then_inc(pt_done, 1)

            def values(n, e):
                pe.wait_ge(pt_split, n * 3 + 3)
                for j in range(QT):
                    w = P * (QT - j)
                    pt = slice(T_COL[j], T_COL[j] + w)
                    last = product(PJ[e][:, P * j:S], (v_hi[:, j], v_lo[:, j]), (pt_hi[e][:, pt], pt_lo[e][:, pt]),
                                   j == 0, j == QT - 1)
                last.then_inc(pv_done, 1)

            def v_transposes(p):
                pe.wait_ge(v_taken, p)
                pe.wait_ge(g_taken, p)
                for j in range(QT):
                    last = pe.transpose(PJ[1][:, P * j:P * j + P], v_t[:, P * j:P * j + P], ident[:])
                last.then_inc(vt_done, 1)

            def attention_rest(p):
                pe.wait_ge(v_split, p)
                values(p * 2 - 2, 0)
                values(p * 2 - 1, 1)

            def pair(p, prev):
                u = p * PER_PAIR + U_MIX
                if prev:
                    pe.wait_ge(s_taken, p * 6)
                tile(u, SB[0], (lambda: v_transposes(p)) if prev else None)
                if prev:
                    attention_rest(p)
                    pe.wait_ge(gates_taken, p * 2)
                else:
                    pe.wait_ge(sq_added, KT)
                    channel_sum(SB[2], acc[:])
                tile(u + 2, SB[1])
                if prev:
                    pe.wait_ge(ya_taken, p * 2 - 1)
                else:
                    pe.wait_ge(f_taken, 1)
                tile(u + 4, PJ[0])
                pe.wait_ge(q_split, p + 1)
                pe.wait_ge(k_split, p + 1)
                scores(p * 2, 0)
                if prev:
                    pe.wait_ge(ya_taken, p * 2)
                tile(u + 6, PJ[1])
                transposes(p * 2, 0)
                pe.wait_ge(s_taken, p * 6 + 3)
                scores(p * 2 + 1, 1)
                pe.wait_ge(x_taken, p + 1)
                tile(u + 8, PJ[0])
                pe.wait_ge(s_taken, p * 6 + 6)
                pe.wait_ge(gw_split, p + 1)
                pe.wait_ge(xc_split, p + 1)
                for g in range(2):
                    last = product(SB[1 + g][:], (gw_hi[:, g], gw_lo[:, g]), (xc_hi[:], xc_lo[:]), True, True)
                last.then_inc(gates_done, 1)
                transposes(p * 2 + 1, 1)

            def after_split(n):
                return lambda k: pe.wait_ge(act_split, n + k + 1)

            unit(0, 0, 0, PJ[0], True, False, after_split(0))
            unit(1, 1, 1, PJ[0], False, True, after_split(0))
            pe.wait_ge(consts_set, 3)
            pair(0, False)
            with pe.Fori(1, NP) as p:
                pair(p, True)
            v_transposes(NP)
            attention_rest(NP)

            def out_tile(t, s, first=False):
                u = t * 2 + U_OUT
                a, b = ((SB[0], SB[1]), (PT[0], PT[1]))[s]
                unit(u, 0, 0, a, True, True, after_split(KT) if first else None)
                unit(u + 1, 1, 1, b, True, True, after_split(KT) if first else None)

            pe.wait_ge(s_taken, 6 * NP)
            pe.wait_ge(gates_taken, 2 * NP)
            out_tile(0, 0, True)
            pe.wait_ge(ynorm_ready, 2)
            channel_sum(SB[2], acc[:])
            channel_sum(PT[2], acc_b[:])
            out_tile(1, 1)
            with pe.Fori(1, KT // 2) as i:
                pe.wait_ge(wo_taken, i * 2 - 1)
                out_tile(i * 2, 0)
                pe.wait_ge(wo_taken, i * 2)
                out_tile(i * 2 + 1, 1)
            pe.wait_ge(osum_ready, 1)
            pe.wait_ge(std_done, 3)
            pe.matmul(SB[2][:], ones[:], acc[:], start=True, stop=True).then_inc(sum_done, 1)
            pe.wait_ge(sum_done, 4)
            pe.sem_inc(x1sq_used, 1)

            pe.wait_ge(std_done, 4)
            for half in range(2):
                pe.wait_ge(split_done, U_FF + half + 1)
                for i in range(UK):
                    k = half * UK + i
                    pe.wait_ge(act_split, 2 * KT + k + 1)
                    last = product(PJ[0][:], w_tile(half, i), (act_hi[:, k], act_lo[:, k]), k == 0, k == KT - 1)
                    if i == UK - 1:
                        last.then_inc(unit_used, 1)
                    pe.wait_ge(x1sq_done, k + 1)
                    last = pe.matmul(SB[2][:], ones[:], sq[:, 0], start=(k == 0), stop=(k == KT - 1))
                    last.then_inc(x1sq_used if k < KT - 1 else sum_done, 1)
            tile(U_FF + 2, PJ[1])
            with pe.Fori(1, FT) as j:
                pe.wait_ge(gate_taken, j)
                tile(j * 4 + U_FF, PJ[0])
                pe.wait_ge(up_taken, j)
                tile(j * 4 + (U_FF + 2), PJ[1])

            def down_unit(n, s, out_banks, start=False, stop=False):
                pe.wait_ge(split_done, n + (U_DOWN + 1))
                pe.wait_ge(h_split, n + 1)
                for kt in range(2):
                    tok = slice(S * kt, S * kt + S)
                    for i, bank in enumerate(out_banks):
                        last = product(bank[:], w_tile(s, 4 * kt + i), (h_hi[:, s, tok], h_lo[:, s, tok]),
                                       start and kt == 0, stop and kt == 1)
                last.then_inc(unit_used, 1)

            pe.wait_ge(std_done, 5)
            for g in range(GROUPS):
                n, out_banks = g * PER_GROUP, DOWN_BANKS[g % 2]
                if g == 1:
                    pe.wait_ge(up_taken, FT)
                at_least(pe, wd_taken, 4 * (g - 1))
                down_unit(n, 0, out_banks, start=True)
                down_unit(n + 1, 1, out_banks)
                with pe.Fori(1, PER_GROUP // 2 - 1) as t:
                    down_unit(t * 2 + n, 0, out_banks)
                    down_unit(t * 2 + (n + 1), 1, out_banks)
                down_unit(n + PER_GROUP - 2, 0, out_banks)
                down_unit(n + PER_GROUP - 1, 1, out_banks, stop=True)
            pe.wait_ge(wdsum_ready, 1)
            channel_sum(SB[2], acc[:])


def kernel(x, norm_mix_pre, w_in, b_forget, conv_rnn_w, conv_rnn_b, w_rg_a, b_rg_a, w_rg_x, b_rg_x, rg_lambda,
           norm_attn_out, norm_rnn_out, w_out, norm_mix_post, norm_ffn_pre, w_gate, w_up, conv_ffn_w, conv_ffn_b,
           w_down, norm_ffn_post):
    import numpy as np
    import concourse.bacc as bacc
    from concourse.bass_utils import run_bass_kernel_spmd

    def tiles(v):
        return np.asarray(v).reshape(-1, P).T

    xT = np.ascontiguousarray(np.asarray(x)[0].T.reshape(KT, P, S).transpose(1, 0, 2))
    par = np.zeros((P, NPAR), np.float32)
    for name, v in (("g_pre", norm_mix_pre), ("conv_w", conv_rnn_w), ("conv_b", conv_rnn_b), ("b_a", b_rg_a),
                    ("b_x", b_rg_x), ("lam", rg_lambda), ("g_y", norm_attn_out), ("g_post", norm_mix_post),
                    ("g_ffn", norm_ffn_pre), ("ffn_w", conv_ffn_w), ("ffn_b", conv_ffn_b),
                    ("g_ffn_post", norm_ffn_post)):
        t = tiles(v)
        par[:, COLS[name]:COLS[name] + t.shape[1]] = t
    par[:, COLS["g_y"] + NP:COLS["g_y"] + KT] = tiles(norm_rnn_out)
    par[0:2 * NP, COLS["b_forget"]] = np.asarray(b_forget)[0]

    weights = np.zeros((NU, P, UW), np.float32)

    def units(w):
        w = np.asarray(w)
        return w.reshape(2, UK, P, -1, P).transpose(3, 0, 2, 1, 4).reshape(-1, 2, P, UW)

    win = np.asarray(w_in)[0]
    f0, x0 = 3 * DA, 3 * DA + 2 * NP
    weights[0:2].reshape(2, P, UK, P)[:, :, :, 0:2 * NP] = win[:, f0:x0].reshape(2, UK, P, 2 * NP).transpose(0, 2, 1, 3)
    mixed = weights[U_MIX:U_OUT].reshape(NP, 5, 2, P, UW)
    for i, c in enumerate((0, DA, x0, x0 + DA, 2 * DA)):
        mixed[:, i] = units(win[:, c:c + DA])
    weights[U_OUT:U_FF] = units(w_out[0]).reshape(-1, P, UW)
    hidden = weights[U_FF:U_DOWN].reshape(FT, 2, 2, P, UW)
    hidden[:, 0] = units(w_gate[0])
    hidden[:, 1] = units(w_up[0])
    weights[U_DOWN:] = np.asarray(w_down)[0].reshape(PER_GROUP, 2, P, GROUPS, 4 * P).transpose(3, 0, 2, 1, 4).reshape(
        -1, P, UW)

    gate_w = np.zeros((NP, P, 2, P), np.float32)
    for g, w in enumerate((w_rg_a, w_rg_x)):
        w = np.asarray(w)[0].reshape(NP, 2, HD, HD)
        for e in range(2):
            gate_w[:, HD * e:HD * e + HD, g, HD * e:HD * e + HD] = w[:, e]

    nc = bacc.Bacc("TRN2", target_bir_lowering=False, num_devices=1)
    arrays = {"xT": xT, "params": par, "weights": weights, "gate_w": gate_w}
    aps = [nc.dram_tensor(n, a.shape, F32, kind="ExternalInput").ap() for n, a in arrays.items()]
    out = nc.dram_tensor("out", (P, KT, S), F32, kind="ExternalOutput").ap()
    block_kernel(nc, *aps, out)
    r = run_bass_kernel_spmd(nc, [arrays], core_ids=[0])
    got = np.asarray(r.results[0]["out"])
    return np.ascontiguousarray(got.transpose(1, 0, 2).reshape(D, S).T)[None]
```

```python
from contextlib import ExitStack

import concourse.bass as bass
from concourse import mybir

F32 = mybir.dt.float32
F32R = mybir.dt.float32r
ALU = mybir.AluOpType
ACT = mybir.ActivationFunctionType
AXX = mybir.AxisListType.X

P = 128
S = 512
D = 2048
KT = D // P
DA = 1024
NP = DA // P
HD = 64
RG_C = 8.0
FF = 3 * D
FT = FF // P
QT = S // P
UK = 8
UW = UK * P
EPS = 1e-6
SCALE = HD ** -0.5
NEG = -1e30

PER_PAIR = 10
U_MIX = 2
U_OUT = U_MIX + PER_PAIR * NP
U_FF = U_OUT + 2 * KT
U_DOWN = U_FF + 4 * FT
GROUPS = 4
PER_GROUP = FT // 2
NU = U_DOWN + GROUPS * PER_GROUP

COLS = {}
_n = 0
for _name, _w in (("g_pre", KT), ("conv_w", 4 * NP), ("conv_b", NP), ("b_a", NP), ("b_x", NP), ("lam", NP),
                  ("g_y", KT), ("g_post", KT), ("g_ffn", KT), ("ffn_w", 3 * FT), ("ffn_b", FT),
                  ("g_ffn_post", KT), ("b_forget", 1)):
    COLS[_name] = _n
    _n += _w
NPAR = _n

S_SEGS = [(3, 0, 0, 0), (2, 1, 0, 512), (0, 1, 384, 896), (1, 2, 0, 1024)]
S_COL = {q: c for q, _, _, c in S_SEGS}
T_SEGS = [(0, 0, 0, 0), (1, 1, 0, 512), (3, 1, 384, 896), (2, 2, 0, 1024)]
T_COL = {j: c for j, _, _, c in T_SEGS}
T_BANKS = [(0, 512), (512, 512), (1024, 256)]
CAUSAL = 1280
X_CHUNKS = ((0, 1), (1, 4), (4, 8), (8, 10), (10, 12), (12, 14), (14, KT))
Y_ORDER = (0, 1, 2, 3, 4, 5, 6, 8, 9, 10, 11, 12, 13, 14, 7, 15)
Y_POOL = (4, 5, 6, 8, 9, 10, 11, 12, 13, 14)
Y_VECTOR = tuple(k for k in range(KT) if k not in Y_POOL)
AFTER_Y = KT + len(Y_VECTOR)
OUT_POOL = 5
LOG1P = [1.0 / n for n in (15, 13, 11, 9, 7, 5, 3)]


def word(t):
    return t.bitcast(F32)


def at_least(eng, sem, value):
    if isinstance(value, int) and value <= 0:
        return
    eng.wait_ge(sem, value)


class Chain:

    def __init__(self, eng, sem):
        self.eng, self.sem, self.base, self.n = eng, sem, 0, 0

    def __call__(self, instruction):
        self.n += 1
        instruction.then_inc(self.sem, 1)
        self.eng.wait_ge(self.sem, self.base + self.n)

    def loop(self, i, links):
        self.start, self.links = self.base + self.n, links
        self.base, self.n = self.start + i * links, 0

    def end_loop(self, rounds):
        assert self.n == self.links, self.n
        self.base, self.n = self.start + rounds * self.links, 0


def block_kernel(nc, xT, par_d, weights, gate_w, out):
    negc_d = nc.dram_tensor("negc", [2 * NP, S], F32, kind="Internal").ap()
    x1_d = nc.dram_tensor("x1_spill", [P, KT, S], F32, kind="Internal").ap()

    with ExitStack() as ctx:
        def sb_in(stack, name, shape, dt=F32):
            return stack.enter_context(nc.sbuf_tensor(name, [P, *shape], dt))

        def sb(name, shape, dt=F32):
            return sb_in(ctx, name, shape, dt)

        def sem(name):
            return ctx.enter_context(nc.semaphore(name))

        par = sb("par", [NPAR])
        raw = sb("raw", [2, UW])
        w_hi = sb("w_hi", [2, UW], F32R)
        w_lo = sb("w_lo", [2, UW], F32R)
        ones = sb("ones", [P])
        eps = sb("eps", [1])
        rms = sb("rms", [S])
        sq = sb("sq", [2, S])
        std = sq[:, 1]
        acc = sb("acc", [S])
        ident = sb("ident", [P])
        cols = sb("cols", [2, QT])
        banks = [ctx.enter_context(nc.psum_tensor(f"bank{i}", [P, S], F32)) for i in range(8)]
        PJ, SB, PT = banks[0:2], banks[2:5], banks[5:8]
        DOWN_BANKS = (banks[4:8], banks[0:4])

        region_a = ExitStack()
        act_hi = sb_in(region_a, "act_hi", [KT, S], F32R)
        act_lo = sb_in(region_a, "act_lo", [KT, S], F32R)
        region_a.close()
        x1_back = sb("x1_back", [KT, S])
        yd = sb("yd", [KT - 4, S])
        h_hi1 = sb("h_hi1", [2 * S], F32R)
        h_lo1 = sb("h_lo1", [2 * S], F32R)
        mix = ExitStack()
        y_t = sb_in(mix, "y_t", [KT, S])
        v_t = sb_in(mix, "v_t", [S])
        xr = sb_in(mix, "xr", [S + 4])
        xc = sb_in(mix, "xc", [S])
        xc_hi = sb_in(mix, "xc_hi", [S], F32R)
        xc_lo = sb_in(mix, "xc_lo", [S], F32R)
        gel = sb_in(mix, "gel", [S])
        rg = sb_in(mix, "rg", [S])
        ig = sb_in(mix, "ig", [S])
        tt = sb_in(mix, "tt", [S])
        ae = sb_in(mix, "ae", [S])
        w1 = sb_in(mix, "w1", [S])
        w2 = sb_in(mix, "w2", [S])
        st = sb_in(mix, "st", [S])
        ev = sb_in(mix, "ev", [S])
        q_hi = sb_in(mix, "q_hi", [S], F32R)
        q_lo = sb_in(mix, "q_lo", [S], F32R)
        k_hi = sb_in(mix, "k_hi", [S], F32R)
        k_lo = sb_in(mix, "k_lo", [S], F32R)
        v_hi = sb_in(mix, "v_hi", [QT, P], F32R)
        v_lo = sb_in(mix, "v_lo", [QT, P], F32R)
        pt_hi = [sb_in(mix, f"pt_hi{e}", [CAUSAL], F32R) for e in range(2)]
        pt_lo = [sb_in(mix, f"pt_lo{e}", [CAUSAL], F32R) for e in range(2)]
        sm = sb_in(mix, "sm", [CAUSAL])
        negc = sb_in(mix, "negc_sb", [2, S])
        pick = sb_in(mix, "pick", [2, P])
        gw = sb_in(mix, "gw", [2, P])
        gw_hi = sb_in(mix, "gw_hi", [2, P], F32R)
        gw_lo = sb_in(mix, "gw_lo", [2, P], F32R)
        stats = sb_in(mix, "stats", [3, QT])
        lam4 = sb_in(mix, "lam4", [NP])
        lam8 = sb_in(mix, "lam8", [NP])
        lt = sb_in(mix, "lt", [6, NP])
        mask = sb_in(mix, "mask", [P])
        acc_b = sb_in(mix, "acc_b", [S])
        mix.close()
        start = ExitStack()
        x_sb = sb_in(start, "x_sb", [KT, S])
        start.close()
        outp = ExitStack()
        sb_in(outp, "y_t_place", [KT, S])
        x1 = sb_in(outp, "x1", [KT, S])
        og = sb_in(outp, "og", [KT, S])
        rms_a = sb_in(outp, "rms_a", [S])
        rms_b = sb_in(outp, "rms_b", [S])
        o1 = sb_in(outp, "o1", [S])
        o2 = sb_in(outp, "o2", [S])
        outp.close()
        ffn = ExitStack()
        h_t = sb_in(ffn, "h_t", [FT, S])
        gb = sb_in(ffn, "gb", [S + 2])
        cv = sb_in(ffn, "cv", [S])
        h_hi = (sb_in(ffn, "h_hi0", [2 * S], F32R), h_hi1)
        h_lo = (sb_in(ffn, "h_lo0", [2 * S], F32R), h_lo1)
        ffn.close()
        tail = ExitStack()
        yd_last = sb_in(tail, "yd_last", [4, S])
        sq_last = sb_in(tail, "sq_last", [4, S])
        tail.close()

        names = """par_landed hi_done split_done unit_used consts_set zeros_set
            act_hi_done act_split rnn_split sq_done sq_added sq_added_b sums_cleared sum_done std_done rms_set
            f_taken f_negabs f_exp negc_ready negc_stored negc_spread negc_copied
            negc_landed lam_negabs lam_exp lam_ready
            gw_landed gw_hi_done gw_split q_taken q_hi_done q_split k_taken k_hi_done k_split
            v_taken vt_done v_hi_done v_split x_taken xc_done xc_hi_done xc_split g_taken gel_done
            qk_done s_taken max_done exp_done probs_ready pt_done pt_hi_done pt_split pv_done ya_taken
            gates_done gates_taken gate_funcs yr_done ysq_done ynorm_ready y_scaled wo_taken o_done osq_done osum_ready
            res_landed og_scaled x1_done x1_stored x1_landed x1sq_done x1sum_ready x1sum_b_ready
            gate_taken conv_done gelu_done up_taken h_done h_hi_done h_split
            wd_taken wdsq_done wdsum_ready yd_last_done diag_done spread_done yd_scaled yd_scaled_b
            out_ready out_ready_b stored dve_chain""".split()
        (par_landed, hi_done, split_done, unit_used, consts_set, zeros_set,
         act_hi_done, act_split, rnn_split, sq_done, sq_added, sq_added_b, sums_cleared, sum_done, std_done, rms_set,
         f_taken, f_negabs, f_exp, negc_ready, negc_stored, negc_spread, negc_copied,
         negc_landed, lam_negabs, lam_exp, lam_ready,
         gw_landed, gw_hi_done, gw_split, q_taken, q_hi_done, q_split, k_taken, k_hi_done, k_split,
         v_taken, vt_done, v_hi_done, v_split, x_taken, xc_done, xc_hi_done, xc_split, g_taken, gel_done,
         qk_done, s_taken, max_done, exp_done, probs_ready, pt_done, pt_hi_done, pt_split, pv_done, ya_taken,
         gates_done, gates_taken, gate_funcs, yr_done, ysq_done, ynorm_ready, y_scaled,
         wo_taken, o_done, osq_done, osum_ready,
         res_landed, og_scaled, x1_done, x1_stored, x1_landed, x1sq_done, x1sum_ready, x1sum_b_ready,
         gate_taken, conv_done, gelu_done, up_taken, h_done, h_hi_done, h_split,
         wd_taken, wdsq_done, wdsum_ready, yd_last_done, diag_done, spread_done, yd_scaled, yd_scaled_b,
         out_ready, out_ready_b, stored, dve_chain) = [sem(n) for n in names]
        x_landed = [sem(f"x_landed{c}") for c in range(len(X_CHUNKS))]
        raw_landed = [sem(f"raw_landed{s}") for s in range(2)]

        def col(name, i=0):
            c = COLS[name] + i
            return par[:, c:c + 1] if isinstance(c, int) else par[:, bass.ds(c, 1)]

        def tile_of(t, i, part=slice(0, P)):
            return t[part, i] if isinstance(i, int) else t[part, bass.ds(i, 1), :].rearrange("p a s -> p (a s)")

        def two_tiles(t, ku):
            return t[:, bass.ds(ku * 2, 2), :].rearrange("p a s -> p (a s)")

        def one_col(t, i):
            return t[:, i:i + 1] if isinstance(i, int) else t[:, bass.ds(i, 1)]

        def flat(t):
            return t[:].rearrange("p a s -> p (a s)")

        def yd_tile(k):
            return yd[:, k] if k < KT - 4 else yd_last[:, k - (KT - 4)]

        block = ctx.enter_context(nc.Block())

        @block.sync
        def _(sp):
            sp.dma_start(par[:], par_d).then_inc(par_landed, 16)
            for c, (k0, k1) in enumerate(X_CHUNKS):
                if c in (0, 2):
                    sp.dma_start(raw[:, c // 2], weights[c // 2]).then_inc(raw_landed[c // 2], 16)
                sp.dma_start(x_sb[:, k0:k1], xT[:, k0:k1]).then_inc(x_landed[c], 16)
            with sp.Fori(1, NU // 2) as t:
                for s in range(2):
                    sp.wait_ge(split_done, t * 2 + (s - 1))
                    sp.dma_start(raw[:, s], weights[bass.ds(t * 2 + s, 1)].rearrange("a p n -> p (a n)")).then_inc(
                        raw_landed[s], 16)
            parts = ((5, 8), (0, 2), (8, 11), (11, 14), (2, 4), (14, 15), (4, 5), (15, 16))
            for k0, k1 in parts:
                if k1 <= OUT_POOL:
                    sp.wait_ge(out_ready_b, k1)
                else:
                    sp.wait_ge(out_ready, k1 - OUT_POOL)
                sp.dma_start(out[:, k0:k1], x1_back[:, k0:k1]).then_inc(stored, 16)
            sp.wait_ge(stored, 16 * len(parts))

        @block.gpsimd
        def _(pool):
            pool.dma_start(gw[:], gate_w[0]).then_inc(gw_landed, 16)
            pool.memset(eps[:], EPS)
            pool.memset(ones[:], 1.0).then_inc(consts_set, 1)
            pool.memset(ident[:], 0.0).then_inc(zeros_set, 1)
            pool.memset(mask[:], 0.0).then_inc(zeros_set, 1)
            pool.memset(xr[:, 0:4], 0.0).then_inc(zeros_set, 1)
            pool.memset(acc[:], 0.0).then_inc(zeros_set, 1)
            pool.memset(acc_b[:], 0.0).then_inc(zeros_set, 1)
            pool.memset(pick[:], 0.0).then_inc(zeros_set, 1)
            pool.wait_ge(zeros_set, 6)
            pool.affine_select(out=ident[:], in_=ident[:], compare_op=ALU.not_equal, fill=1.0, base=0,
                               pattern=[[-1, P]], channel_multiplier=1).then_inc(consts_set, 1)
            for e in range(2):
                pool.affine_select(out=pick[:, e], in_=pick[:, e], compare_op=ALU.not_equal, fill=1.0, base=-e,
                                   pattern=[[0, P]], channel_multiplier=1).then_inc(consts_set, 1)
            pool.affine_select(out=mask[:], in_=mask[:], compare_op=ALU.is_ge, fill=NEG, base=0,
                               pattern=[[-1, P]], channel_multiplier=1).then_inc(consts_set, 1)
            for i in range(KT // 2):
                pool.wait_ge(sq_done, 2 * i + 2)
                at_least(pool, sq_added, i)
                pool.tensor_tensor(acc[:], acc[:], x_sb[:, 2 * i + 1], ALU.add).then_inc(sq_added, 1)
            pool.wait_ge(sum_done, 1)
            pool.memset(acc[:], 0.0).then_inc(sums_cleared, 1)
            pool.memset(acc_b[:], 0.0).then_inc(sums_cleared, 1)
            pool.wait_ge(negc_ready, 1)
            pool.dma_start(negc_d, tt[0:2 * NP]).then_inc(negc_stored, 16)
            pool.wait_ge(negc_stored, 16)
            with pool.Fori(1, NP) as p:
                pool.wait_ge(gw_split, p)
                pool.dma_start(gw[:], gate_w[bass.ds(p, 1)].rearrange("a p m n -> p (a m) n")).then_inc(gw_landed, 16)
                pool.wait_ge(s_taken, p * 6)
                pool.dma_start(negc[:], negc_d[bass.ds(p * 2, 2)].partition_broadcast(P)).then_inc(negc_landed, 16)
            pool.wait_ge(ysq_done, 2 * (NP - 1))
            for k in Y_POOL:
                pool.tensor_scalar(y_t[:, k], y_t[:, k], col("g_y", k), None, ALU.mult).then_inc(y_scaled, 1)
            for k in Y_POOL:
                pool.wait_ge(act_hi_done, KT + Y_ORDER.index(k) + 1)
                pool.tensor_tensor(act_lo[:, k], y_t[:, k], word(act_hi[:, k]), ALU.subtract).then_inc(rnn_split, 1)
            pool.wait_ge(ynorm_ready, 2)
            pool.wait_ge(act_split, AFTER_Y)
            for k in range(KT):
                pool.wait_ge(unit_used, U_OUT + k)
                pool.dma_start(x1[:, k], xT[:, k]).then_inc(res_landed, 16)
            pool.wait_ge(rms_set, 4)
            with pool.Fori(1, KT) as k:
                pool.tensor_tensor(tile_of(og, k), tile_of(og, k), rms[:], ALU.mult).then_inc(og_scaled, 1)
            for k in range(1, KT // 2):
                pool.wait_ge(x1sq_done, k + 1)
                at_least(pool, x1sum_ready, k - 1)
                pool.tensor_tensor(acc[:], og[:, 0] if k == 1 else acc[:], og[:, k], ALU.add).then_inc(x1sum_ready, 1)
            pool.wait_ge(x1_stored, 16 * KT)
            for k in range(KT):
                pool.wait_ge(unit_used, U_DOWN + k)
                pool.dma_start(x1_back[:, k], x1_d[:, k]).then_inc(x1_landed, 16)
            pool.wait_ge(x1_landed, 16 * KT)
            pool.wait_ge(wdsum_ready, 1)
            pool.wait_ge(rms_set, 6)
            for k in range(OUT_POOL + 1):
                if k < OUT_POOL:
                    pool.tensor_tensor(yd[:, k], yd[:, k], rms[:], ALU.mult).then_inc(yd_scaled_b, 1)
                if k:
                    pool.wait_ge(yd_scaled_b, k)
                    pool.tensor_tensor(x1_back[:, k - 1], x1_back[:, k - 1], yd[:, k - 1], ALU.add).then_inc(
                        out_ready_b, 1)

        @block.scalar
        def _(act):
            def split(u, s):
                act.wait_ge(raw_landed[s], (u - s) * 8 + 16)
                at_least(act, unit_used, u - 1)
                act.activation(w_hi[:, s], raw[:, s], ACT.Copy).then_inc(hi_done, 1)

            def split_h(n, s, ku):
                if s or not isinstance(n, int) or n:
                    act.wait_ge(unit_used, n + (U_DOWN - 1))
                act.activation(h_hi[s][:], two_tiles(h_t, ku), ACT.Copy).then_inc(h_hi_done, 1)

            def root(n, bank, dst, width=D):
                act.wait_ge(sum_done, n)
                act.activation(dst, bank[:], ACT.Sqrt, scale=1.0 / width, bias=eps[:, 0:1]).then_inc(std_done, 1)

            def column_roots(n, sums, spread):
                act.wait_ge(sum_done, n)
                act.activation(cols[:, 0], sums[:, 0:QT], ACT.Sqrt, scale=1.0 / D, bias=eps[:, 0:1]).then_inc(
                    std_done, 1)
                act.wait_ge(spread_done, 1)
                act.activation(rms[:], spread[:], ACT.Copy).then_inc(rms_set, 1)

            def pt_his(n, e):
                for b, (c, w) in enumerate(T_BANKS):
                    act.wait_ge(pt_done, n * 3 + (b + 1))
                    act.activation(pt_hi[e][:, c:c + w], PT[b][:, 0:w], ACT.Copy).then_inc(pt_hi_done, 1)

            def exps(n):
                for i, (qt, _, _, c) in enumerate(S_SEGS):
                    act.wait_ge(max_done, n * 4 + (i + 1))
                    seg = sm[:, c:c + P * (qt + 1)]
                    act.activation(seg, seg, ACT.Exp, bias=stats[:, 0, i:i + 1],
                                   accum_out=stats[:, 1, i:i + 1]).then_inc(exp_done, 1)

            def gates(p):
                act.wait_ge(gates_done, p)
                act.activation(rg[:], SB[1][:], ACT.Sigmoid, bias=col("b_a", p - 1)).then_inc(gates_taken, 1)
                act.activation(ig[:], SB[2][:], ACT.Sigmoid, bias=col("b_x", p - 1)).then_inc(gates_taken, 1)

            def gate_functions(p):
                act.wait_ge(gates_taken, p * 2)
                act.activation(tt[:], rg[:], ACT.Tanh, scale=one_col(lam4, p - 1)).then_inc(gate_funcs, 1)
                act.activation(ae[:], rg[:], ACT.Exp, scale=one_col(lam8, p - 1)).then_inc(gate_funcs, 1)
                act.wait_ge(gate_funcs, p * 3 - 1)
                act.activation(st[:], tt[:], ACT.Sqrt).then_inc(gate_funcs, 1)

            def v_his(p):
                act.wait_ge(vt_done, p)
                act.activation(flat(v_hi), PJ[1][:], ACT.Copy).then_inc(v_hi_done, 1)

            def y_squares(p):
                act.wait_ge(ya_taken, p * 2)
                act.activation(sq[:, 0], tile_of(y_t, p - 1), ACT.Square).then_inc(ysq_done, 1)
                act.wait_ge(yr_done, p)
                act.activation(sq[:, 1], tile_of(y_t, p + (NP - 1)), ACT.Square).then_inc(ysq_done, 1)

            def pair(p, prev):
                u = p * PER_PAIR + U_MIX
                split(u + 1, 1)
                if not prev:
                    x_squares(4, 10)
                if prev:
                    gates(p)
                    pt_his(p * 2 - 1, 1)
                split(u + 2, 0)
                if prev:
                    v_his(p)
                    gate_functions(p)
                else:
                    x_squares(10, KT)
                split(u + 3, 1)
                if not prev:
                    root(1, SB[2], std)
                if not prev:
                    split(u + 4, 0)
                    act.wait_ge(f_negabs, 1)
                    act.activation(w1[0:2 * NP], w1[0:2 * NP], ACT.Exp).then_inc(f_exp, 1)
                act.wait_ge(q_taken, p + 1)
                act.activation(q_hi[:], ev[:], ACT.Copy).then_inc(q_hi_done, 1)
                if prev:
                    split(u + 4, 0)
                split(u + 5, 1)
                if prev:
                    y_squares(p)
                act.wait_ge(k_taken, p + 1)
                act.activation(k_hi[:], ev[:], ACT.Copy).then_inc(k_hi_done, 1)
                act.wait_ge(gw_landed, p * 16 + 16)
                act.activation(gw_hi[:], gw[:], ACT.Copy).then_inc(gw_hi_done, 1)
                split(u + 6, 0)
                split(u + 7, 1)
                if not prev:
                    act.wait_ge(negc_spread, 1)
                    for e in range(2):
                        act.activation(negc[:, e], PT[e][:], ACT.Copy).then_inc(negc_copied, 1)
                exps(p * 2)
                split(u + 8, 0)
                act.wait_ge(xc_done, p + 1)
                act.activation(xc_hi[:], xc[:], ACT.Copy).then_inc(xc_hi_done, 1)
                split(u + 9, 1)
                pt_his(p * 2, 0)
                exps(p * 2 + 1)
                split(u + 10, 0)
                act.wait_ge(g_taken, p + 1)
                act.activation(gel[:], ev[:], ACT.Gelu_apprx_tanh).then_inc(gel_done, 1)

            act.wait_ge(consts_set, 1)
            act.wait_ge(par_landed, 16)
            act.wait_ge(lam_negabs, 1)
            act.activation(lt[:, 1], lt[:, 0], ACT.Exp).then_inc(lam_exp, 1)
            split(0, 0)
            for c, (k0, k1) in enumerate(X_CHUNKS):
                act.wait_ge(x_landed[c], 16)
                for k in range(k0, k1):
                    act.activation(act_hi[:, k], x_sb[:, k], ACT.Copy, scale=col("g_pre", k)).then_inc(act_hi_done, 1)
                    if k == UK - 2:
                        split(1, 1)

            def x_squares(k0, k1):
                for k in range(k0, k1):
                    act.wait_ge(act_split, k + 1)
                    act.activation(x_sb[:, k], x_sb[:, k], ACT.Square).then_inc(sq_done, 1)

            split(2, 0)
            x_squares(0, 4)
            pair(0, False)
            act.wait_ge(lam_ready, 1)
            act.wait_ge(negc_stored, 16)
            with act.Fori(1, NP) as p:
                pair(p, True)

            def y_hi(k):
                if k in Y_POOL:
                    act.wait_ge(y_scaled, Y_POOL.index(k) + 1)
                    act.activation(act_hi[:, k], y_t[:, k], ACT.Copy).then_inc(act_hi_done, 1)
                else:
                    act.activation(act_hi[:, k], y_t[:, k], ACT.Copy, scale=col("g_y", k)).then_inc(act_hi_done, 1)

            act.wait_ge(unit_used, U_OUT)
            for k in Y_ORDER[:3]:
                y_hi(k)
            pt_his(2 * NP - 1, 1)
            v_his(NP)
            gates(NP)
            for k in Y_ORDER[3:8]:
                y_hi(k)
            gate_functions(NP)
            for k in Y_ORDER[8:14]:
                y_hi(k)
            act.wait_ge(ya_taken, 2 * NP)
            y_hi(NP - 1)
            split(U_OUT + 1, 1)
            act.wait_ge(yr_done, NP)
            y_hi(KT - 1)
            y_squares(NP)
            split(U_OUT + 2, 0)
            split(U_OUT + 3, 1)
            root(2, SB[2], rms_a[:], DA)
            root(3, PT[2], rms_b[:], DA)

            def out_square(t):
                act.wait_ge(o_done, t + 1)
                act.activation(sq[:, 0], o1[:], ACT.Square).then_inc(osq_done, 1)

            split(U_OUT + 4, 0)
            out_square(0)
            with act.Fori(2, KT) as t:
                split(t * 2 + (U_OUT + 1), 1)
                out_square(t - 1)
                split(t * 2 + (U_OUT + 2), 0)
            out_square(KT - 1)
            split(U_FF + 1, 1)
            column_roots(4, SB[2], PT[2])

            with act.Fori(0, KT) as k:
                act.wait_ge(x1_done, k + 1)
                act.activation(tile_of(act_hi, k), tile_of(x1, k), ACT.Copy, scale=col("g_ffn", k)).then_inc(
                    act_hi_done, 1)
                act.activation(tile_of(og, k), tile_of(x1, k), ACT.Square).then_inc(x1sq_done, 1)
                act.dma_start(tile_of(x1_d, k), tile_of(x1, k)).then_inc(x1_stored, 16)

            def gelu_gate(j):
                act.wait_ge(conv_done, j + 1)
                act.activation(cv[:], cv[:], ACT.Gelu_apprx_tanh).then_inc(gelu_done, 1)

            split(U_FF + 2, 0)
            split(U_FF + 3, 1)
            split(U_FF + 4, 0)
            root(5, SB[2], std)
            split(U_FF + 5, 1)
            gelu_gate(0)
            split(U_FF + 6, 0)
            split(U_FF + 7, 1)
            gelu_gate(1)
            split(U_FF + 8, 0)
            with act.Fori(2, FT) as j:
                split(j * 4 + (U_FF + 1), 1)
                split(j * 4 + (U_FF + 2), 0)
                split(j * 4 + (U_FF + 3), 1)
                gelu_gate(j)
                split(j * 4 + (U_FF + 4), 0)

            act.wait_ge(h_done, 2)
            split_h(0, 0, 0)
            act.wait_ge(h_done, FT)

            def both(n, s, ku):
                split(n + U_DOWN, s)
                split_h(n, s, ku)

            def down_square(g, i):
                act.wait_ge(wd_taken, 4 * g + i + 1)
                act.activation(sq[:, 0], sq[:, 1], ACT.Square).then_inc(wdsq_done, 1)

            for g in range(GROUPS):
                n = g * PER_GROUP
                for i in range(4):
                    both(n + 1 + i, (i + 1) % 2, 1 + i)
                    if g:
                        down_square(g - 1, i)
                with act.Fori(2, PER_GROUP // 2 - 1) as t:
                    both(t * 2 + (n + 1), 1, t * 2 + 1)
                    both(t * 2 + (n + 2), 0, t * 2 + 2)
                both(n + PER_GROUP - 1, 1, PER_GROUP - 1)
                if g < GROUPS - 1:
                    both(n + PER_GROUP, 0, 0)
            act.wait_ge(unit_used, NU)
            for i in range(4):
                act.activation(sq_last[:, i], DOWN_BANKS[1][i][:], ACT.Square).then_inc(wdsq_done, 1)

            def last_tile(i):
                act.activation(yd_last[:, i], DOWN_BANKS[1][i][:], ACT.Copy,
                               scale=col("g_ffn_post", KT - 4 + i)).then_inc(yd_last_done, 1)

            last_tile(0)
            last_tile(1)
            root(6, SB[2], std)
            last_tile(2)
            last_tile(3)

        @block.vector
        def _(dve):
            chain = Chain(dve, dve_chain)

            def split(u, s):
                dve.wait_ge(hi_done, u + 1)
                dve.tensor_tensor(w_lo[:, s], raw[:, s], word(w_hi[:, s]), ALU.subtract).then_inc(split_done, 1)

            def split_h(n, s, ku):
                dve.wait_ge(h_hi_done, n + 1)
                dve.tensor_tensor(h_lo[s][:], two_tiles(h_t, ku), word(h_hi[s][:]), ALU.subtract).then_inc(h_split, 1)

            def lo_of_scaled(k, src, gain, n):
                dve.wait_ge(act_hi_done, n + 1)
                dve.scalar_tensor_tensor(out=tile_of(act_lo, k), in0=tile_of(src, k), scalar=col(gain, k),
                                         in1=word(tile_of(act_hi, k)), op0=ALU.mult,
                                         op1=ALU.subtract).then_inc(act_split, 1)

            def invert_root(n, dst, src):
                dve.wait_ge(std_done, n)
                dve.reciprocal(dst, src).then_inc(rms_set, 1)
                dve.wait_ge(rms_set, n)

            def invert_columns():
                dve.wait_ge(std_done, 4)
                chain(dve.reciprocal(cols[:, 1], cols[:, 0]))
                shape = [P, QT, P]
                dve.tensor_tensor(sq[:, 0].rearrange("p (a b) -> p a b", a=QT),
                                  ident[:].unsqueeze(1).broadcast_to(shape),
                                  cols[:, 1].unsqueeze(2).broadcast_to(shape), ALU.mult).then_inc(diag_done, 1)

            def log1p_ratio(y, s, z):
                chain(dve.tensor_scalar(s, y, 2.0, None, ALU.add))
                chain(dve.reciprocal(s, s))
                chain(dve.tensor_tensor(s, y, s, ALU.mult))
                chain(dve.tensor_tensor(z, s, s, ALU.mult))

            def log1p_series(s, z, w):
                chain(dve.tensor_scalar(w, z, LOG1P[0], None, ALU.mult))
                for c in LOG1P[1:]:
                    chain(dve.scalar_tensor_tensor(out=w, in0=w, scalar=c, in1=z, op0=ALU.add, op1=ALU.mult))
                chain(dve.scalar_tensor_tensor(out=w, in0=w, scalar=1.0, in1=s, op0=ALU.add, op1=ALU.mult))

            lam = par[:, COLS["lam"]:COLS["lam"] + NP]

            def lambda_terms():
                chain(dve.tensor_scalar(lt[:, 5], lam, -1.0, 0.0, ALU.mult, ALU.max))
                dve.wait_ge(lam_exp, 1)
                log1p_ratio(lt[:, 1], lt[:, 2], lt[:, 3])
                log1p_series(lt[:, 2], lt[:, 3], lt[:, 4])
                chain(dve.scalar_tensor_tensor(out=lt[:, 4], in0=lt[:, 4], scalar=2.0, in1=lt[:, 5], op0=ALU.mult,
                                               op1=ALU.add))
                dve.tensor_scalar(lam4[:], lt[:, 4], RG_C / 2, None, ALU.mult)
                dve.tensor_scalar(lam8[:], lt[:, 4], -RG_C, None, ALU.mult).then_inc(lam_ready, 1)

            H = 2 * NP

            def forget_logits():
                dve.tensor_tensor(v_t[0:H], PJ[0][0:H], rms[0:H], ALU.mult).then_inc(f_taken, 1)
                split(U_MIX + 4, 0)
                dve.wait_ge(f_taken, 1)
                chain(dve.tensor_scalar(v_t[0:H], v_t[0:H], par[0:H, COLS["b_forget"]:COLS["b_forget"] + 1], None,
                                        ALU.add))
                dve.scalar_tensor_tensor(out=w1[0:H], in0=v_t[0:H], scalar=-1.0, in1=v_t[0:H], op0=ALU.mult,
                                         op1=ALU.min).then_inc(f_negabs, 1)

            def forget_ratio():
                dve.wait_ge(f_exp, 1)
                log1p_ratio(w1[0:H], w2[0:H], rg[0:H])

            def forget_series():
                log1p_series(w2[0:H], rg[0:H], ig[0:H])

            def forget_sums():
                chain(dve.memset(st[0:H], 1.0))
                chain(dve.tensor_scalar(v_t[0:H], v_t[0:H], 0.0, None, ALU.min))
                chain(dve.scalar_tensor_tensor(out=v_t[0:H], in0=ig[0:H], scalar=-2.0, in1=v_t[0:H], op0=ALU.mult,
                                               op1=ALU.add))
                dve.tensor_tensor_scan(tt[0:H], st[0:H], v_t[0:H], 0.0, ALU.mult, ALU.subtract).then_inc(
                    negc_ready, 1)

            def pt_los(n, e):
                for b, (c, w) in enumerate(T_BANKS):
                    dve.wait_ge(pt_hi_done, n * 3 + (b + 1))
                    dve.tensor_tensor(pt_lo[e][:, c:c + w], PT[b][:, 0:w], word(pt_hi[e][:, c:c + w]),
                                      ALU.subtract).then_inc(pt_split, 1)

            def logits(n, e, p):
                if e == 0:
                    if isinstance(p, int):
                        dve.wait_ge(negc_copied, 2)
                    else:
                        dve.wait_ge(negc_landed, p * 16)
                for i, (qt, b, bc, c) in enumerate(S_SEGS):
                    w = P * (qt + 1)
                    dve.wait_ge(qk_done, n * 3 + (b + 1))
                    ins = dve.scalar_tensor_tensor(out=sm[:, c:c + w], in0=SB[b][:, bc:bc + w], scalar=SCALE,
                                                   in1=negc[:, e, 0:w], op0=ALU.mult, op1=ALU.add)
                    if i == 1:
                        chain(ins)
                    else:
                        ins.then_inc(s_taken, 1)
                        dve.wait_ge(s_taken, n * 3 + (b + 1))
                    diag = sm[:, c + w - P:c + w]
                    chain(dve.tensor_tensor(diag, diag, mask[:], ALU.add))
                    dve.tensor_reduce(stats[:, 0, i:i + 1], sm[:, c:c + w], AXX, ALU.max, negate=True).then_inc(
                        max_done, 1)

            def probabilities(n):
                dve.wait_ge(exp_done, n * 4 + 4)
                chain(dve.reciprocal(stats[:, 2], stats[:, 1]))
                for i, (qt, _, _, c) in enumerate(S_SEGS):
                    seg = sm[:, c:c + P * (qt + 1)]
                    ins = dve.tensor_scalar(seg, seg, stats[:, 2, i:i + 1], None, ALU.mult)
                ins.then_inc(probs_ready, 1)

            def v_out(p):
                dve.wait_ge(unit_used, p * PER_PAIR + U_MIX)
                dve.tensor_tensor(v_t[:], PJ[0][:], rms[:], ALU.mult).then_inc(v_taken, 1)

            def v_los(p):
                dve.wait_ge(v_hi_done, p)
                dve.tensor_tensor(flat(v_lo), PJ[1][:], word(flat(v_hi)), ALU.subtract).then_inc(v_split, 1)

            def decay(p):
                dve.wait_ge(gate_funcs, p * 3 - 1)
                chain(dve.scalar_tensor_tensor(out=w1[:], in0=ae[:], scalar=1.0, in1=tt[:], op0=ALU.add,
                                               op1=ALU.mult))
                chain(dve.tensor_scalar(w2[:], w1[:], -1.0, 1.0, ALU.mult, ALU.add))
                chain(dve.scalar_tensor_tensor(out=ae[:], in0=tt[:], scalar=0.5, in1=ae[:], op0=ALU.is_ge,
                                               op1=ALU.mult))
                chain(dve.scalar_tensor_tensor(out=w2[:], in0=tt[:], scalar=0.5, in1=w2[:], op0=ALU.is_lt,
                                               op1=ALU.mult))
                chain(dve.tensor_tensor(ae[:], ae[:], w2[:], ALU.add))

            def recurrence(p):
                dve.wait_ge(gate_funcs, p * 3)
                chain(dve.scalar_tensor_tensor(out=w2[:], in0=ae[:], scalar=1.0, in1=st[:], op0=ALU.add,
                                               op1=ALU.mult))
                chain(dve.memset(w2[:, 0:1], 1.0))
                chain(dve.tensor_tensor(w2[:], w2[:], ig[:], ALU.mult))
                chain(dve.tensor_tensor(w1[:], w2[:], xc[:], ALU.mult))
                chain(dve.tensor_tensor_scan(w2[:], ae[:], w1[:], 0.0, ALU.mult, ALU.add))
                dve.wait_ge(gel_done, p)
                dve.tensor_tensor(tile_of(y_t, p + (NP - 1)), w2[:], gel[:], ALU.mult).then_inc(yr_done, 1)

            def attention_out(p):
                for e in range(2):
                    dve.wait_ge(pv_done, p * 2 - 1 + e)
                    h = slice(HD * e, HD * e + HD)
                    dve.tensor_copy(tile_of(y_t, p - 1, h), PJ[e][h, :]).then_inc(ya_taken, 1)

            def add_squares(p, last=False):
                for e, a in enumerate((acc, acc_b)):
                    dve.wait_ge(ysq_done, p * 2 - 1 + e)
                    ins = dve.tensor_tensor(a[:], a[:], sq[:, e], ALU.add)
                    ins.then_inc(ynorm_ready, 1) if last else chain(ins)

            def convolution(p):
                dve.wait_ge(unit_used, p * PER_PAIR + (U_MIX + 6))
                dve.tensor_tensor(xr[:, 4:], PJ[0][:], rms[:], ALU.mult).then_inc(x_taken, 1)
                dve.wait_ge(x_taken, p + 1)
                chain(dve.tensor_scalar(xc[:], xr[:, 4:4 + S], col("conv_w", p + 3 * NP), col("conv_b", p), ALU.mult,
                                        ALU.add))
                for tap in (2, 1, 0):
                    ins = dve.scalar_tensor_tensor(out=xc[:], in0=xr[:, 1 + tap:1 + tap + S],
                                                   scalar=col("conv_w", p + tap * NP), in1=xc[:], op0=ALU.mult,
                                                   op1=ALU.add)
                    chain(ins) if tap else ins.then_inc(xc_done, 1)

            def pair(p, prev):
                u = p * PER_PAIR + U_MIX
                split(u + 1, 1)
                if not prev:
                    add_x_squares(4, 10)
                if prev:
                    v_out(p)
                    pt_los(p * 2 - 1, 1)
                split(u + 2, 0)
                if prev:
                    v_los(p)
                    decay(p)
                else:
                    add_x_squares(10, KT)
                split(u + 3, 1)
                if not prev:
                    invert_root(1, rms[:], std)
                    forget_logits()
                dve.wait_ge(unit_used, u + 2)
                dve.tensor_tensor(ev[:], SB[0][:], rms[:], ALU.mult).then_inc(q_taken, 1)
                if prev:
                    attention_out(p)
                dve.wait_ge(q_hi_done, p + 1)
                dve.tensor_tensor(q_lo[:], ev[:], word(q_hi[:]), ALU.subtract).then_inc(q_split, 1)
                if prev:
                    split(u + 4, 0)
                    recurrence(p)
                split(u + 5, 1)
                if not prev:
                    forget_ratio()
                dve.wait_ge(unit_used, u + 4)
                dve.tensor_tensor(ev[:], SB[1][:], rms[:], ALU.mult).then_inc(k_taken, 1)
                dve.wait_ge(k_hi_done, p + 1)
                dve.tensor_tensor(k_lo[:], ev[:], word(k_hi[:]), ALU.subtract).then_inc(k_split, 1)
                dve.wait_ge(gw_hi_done, p + 1)
                dve.tensor_tensor(gw_lo[:], gw[:], word(gw_hi[:]), ALU.subtract).then_inc(gw_split, 1)
                if prev:
                    add_squares(p)
                split(u + 6, 0)
                if not prev:
                    forget_series()
                split(u + 7, 1)
                if not prev:
                    forget_sums()
                    convolution(p)
                logits(p * 2, 0, p)
                probabilities(p * 2)
                split(u + 8, 0)
                if prev:
                    convolution(p)
                dve.wait_ge(xc_hi_done, p + 1)
                dve.tensor_tensor(xc_lo[:], xc[:], word(xc_hi[:]), ALU.subtract).then_inc(xc_split, 1)
                split(u + 9, 1)
                dve.wait_ge(unit_used, u + 8)
                dve.tensor_tensor(ev[:], PJ[1][:], rms[:], ALU.mult).then_inc(g_taken, 1)
                logits(p * 2 + 1, 1, p)
                pt_los(p * 2, 0)
                split(u + 10, 0)
                probabilities(p * 2 + 1)

            dve.wait_ge(par_landed, 16)
            dve.scalar_tensor_tensor(out=lt[:, 0], in0=lam, scalar=-1.0, in1=lam, op0=ALU.mult,
                                     op1=ALU.min).then_inc(lam_negabs, 1)
            split(0, 0)
            for k in range(KT):
                lo_of_scaled(k, x_sb, "g_pre", k)
                if k == X_CHUNKS[1][1] - 1:
                    lambda_terms()
                if k == UK - 2:
                    split(1, 1)

            def add_x_squares(k0, k1):
                for k in range(k0, k1, 2):
                    dve.wait_ge(sq_done, k + 1)
                    dve.tensor_tensor(acc_b[:], acc_b[:], x_sb[:, k], ALU.add).then_inc(sq_added_b, 1)
                    dve.wait_ge(sq_added_b, k // 2 + 1)

            split(2, 0)
            dve.wait_ge(zeros_set, 5)
            add_x_squares(0, 4)
            dve.wait_ge(consts_set, 5)
            pair(0, False)
            dve.wait_ge(sums_cleared, 2)
            with dve.Fori(1, NP) as p:
                chain.loop(p - 1, 5 + 5 + 2 + 5 + 1 + 3 + 5 + 1)
                pair(p, True)
                chain.end_loop(NP - 1)

            def y_lo(k):
                dve.wait_ge(act_hi_done, KT + Y_ORDER.index(k) + 1)
                dve.scalar_tensor_tensor(out=act_lo[:, k], in0=y_t[:, k], scalar=col("g_y", k), in1=word(act_hi[:, k]),
                                         op0=ALU.mult, op1=ALU.subtract).then_inc(act_split, 1)

            v_out(NP)
            pt_los(2 * NP - 1, 1)
            v_los(NP)
            for k in Y_VECTOR[:-2]:
                y_lo(k)
            decay(NP)
            attention_out(NP)
            y_lo(NP - 1)
            split(U_OUT + 1, 1)
            recurrence(NP)
            y_lo(KT - 1)
            add_squares(NP, True)
            split(U_OUT + 2, 0)
            split(U_OUT + 3, 1)
            invert_root(2, rms_a[:], rms_a[:])
            invert_root(3, rms_b[:], rms_b[:])
            chain(dve.memset(acc[:], 0.0))

            def out_tile(t, s, after_taken=None):
                first, second = ((SB[0], SB[1]), (PT[0], PT[1]))[s]
                dve.wait_ge(unit_used, t * 2 + (U_OUT + 2))
                chain(dve.tensor_tensor(o1[:], first[:], rms_a[:], ALU.mult))
                dve.tensor_tensor(o2[:], second[:], rms_b[:], ALU.mult).then_inc(wo_taken, 1)
                if after_taken:
                    after_taken()
                dve.wait_ge(wo_taken, t + 1)
                dve.tensor_tensor(o1[:], o1[:], o2[:], ALU.add).then_inc(o_done, 1)
                dve.wait_ge(o_done, t + 1)
                dve.tensor_scalar(tile_of(og, t), o1[:], col("g_post", t), None, ALU.mult)
                dve.wait_ge(osq_done, t + 1)
                ins = dve.tensor_tensor(acc[:], acc[:], sq[:, 0], ALU.add)
                ins.then_inc(osum_ready, 1) if isinstance(t, int) and t == KT - 1 else chain(ins)

            out_tile(0, 0, lambda: split(U_OUT + 4, 0))
            with dve.Fori(1, KT // 2) as i:
                chain.loop(i - 1, 4)
                split(i * 4 + (U_OUT + 1), 1)
                out_tile(i * 2 - 1, 1)
                split(i * 4 + (U_OUT + 2), 0)
                split(i * 4 + (U_OUT + 3), 1)
                out_tile(i * 2, 0)
                split(i * 4 + (U_OUT + 4), 0)
                chain.end_loop(KT // 2 - 1)
            out_tile(KT - 1, 1)
            split(U_FF + 1, 1)
            invert_columns()
            dve.wait_ge(res_landed, 16 * KT)

            def x1_tile(k):
                at_least(dve, og_scaled, k)
                dve.tensor_tensor(tile_of(x1, k), tile_of(x1, k), tile_of(og, k), ALU.add).then_inc(x1_done, 1)

            dve.wait_ge(rms_set, 4)
            chain(dve.tensor_tensor(og[:, 0], og[:, 0], rms[:], ALU.mult))
            x1_tile(0)
            with dve.Fori(1, KT) as k:
                x1_tile(k)
                dve.wait_ge(x1_done, k)
                lo_of_scaled(k - 1, x1, "g_ffn", k + (2 * KT - 1))
            dve.wait_ge(x1_done, KT)
            lo_of_scaled(KT - 1, x1, "g_ffn", 3 * KT - 1)

            def gate_tile(j, bank=PJ[0]):
                dve.wait_ge(unit_used, j * 4 + (U_FF + 2))
                dve.tensor_tensor(gb[:, 2:], bank[:], rms[:], ALU.mult).then_inc(gate_taken, 1)
                dve.wait_ge(gate_taken, j + 1)
                chain(dve.tensor_scalar(cv[:], gb[:, 2:2 + S], col("ffn_w", j + 2 * FT), col("ffn_b", j), ALU.mult,
                                        ALU.add))
                chain(dve.scalar_tensor_tensor(out=cv[:], in0=gb[:, 1:1 + S], scalar=col("ffn_w", j + FT), in1=cv[:],
                                               op0=ALU.mult, op1=ALU.add))
                dve.scalar_tensor_tensor(out=cv[:], in0=gb[:, 0:S], scalar=col("ffn_w", j), in1=cv[:],
                                         op0=ALU.mult, op1=ALU.add).then_inc(conv_done, 1)

            def up_tile(j, bank=PJ[1]):
                h = tile_of(h_t, j)
                dve.wait_ge(unit_used, j * 4 + (U_FF + 4))
                dve.tensor_tensor(h, bank[:], rms[:], ALU.mult).then_inc(up_taken, 1)
                dve.wait_ge(up_taken, j + 1)
                dve.wait_ge(gelu_done, j + 1)
                dve.tensor_tensor(h, h, cv[:], ALU.mult).then_inc(h_done, 1)

            split(U_FF + 2, 0)
            for k in range(KT // 2 + 1, KT):
                if k == KT // 2 + 4:
                    split(U_FF + 3, 1)
                dve.wait_ge(x1sq_done, k + 1)
                ins = dve.tensor_tensor(rms_a[:], og[:, k - 1] if k == KT // 2 + 1 else rms_a[:], og[:, k], ALU.add)
                chain(ins) if k < KT - 1 else ins.then_inc(x1sum_b_ready, 1)
            split(U_FF + 4, 0)
            invert_root(5, rms[:], std)
            chain(dve.memset(gb[:, 0:2], 0.0))
            split(U_FF + 5, 1)
            gate_tile(0, PT[0])
            dve.wait_ge(x1_stored, 16 * KT)
            up_tile(0, PT[1])
            split(U_FF + 6, 0)
            split(U_FF + 7, 1)
            gate_tile(1)
            split(U_FF + 8, 0)
            with dve.Fori(2, FT) as j:
                chain.loop(j - 2, 2)
                split(j * 4 + (U_FF + 1), 1)
                up_tile(j - 1)
                split(j * 4 + (U_FF + 2), 0)
                split(j * 4 + (U_FF + 3), 1)
                gate_tile(j)
                split(j * 4 + (U_FF + 4), 0)
                chain.end_loop(FT - 2)
            split_h(0, 0, 0)
            up_tile(FT - 1)
            chain(dve.memset(acc[:], 0.0))

            def both(n, s, ku):
                split(n + U_DOWN, s)
                split_h(n, s, ku)

            def add_down_square(t):
                dve.wait_ge(wdsq_done, t + 1)
                src = sq_last[:, t - (KT - 4)] if t >= KT - 4 else sq[:, 0]
                ins = dve.tensor_tensor(acc[:], acc[:], src, ALU.add)
                ins.then_inc(wdsum_ready, 1) if t == KT - 1 else chain(ins)

            def down_tile(g, i):
                t = 4 * g + i
                if i:
                    add_down_square(t - 1)
                else:
                    dve.wait_ge(unit_used, U_DOWN + (g + 1) * PER_GROUP)
                dve.tensor_copy(sq[:, 1], DOWN_BANKS[g % 2][i][:]).then_inc(wd_taken, 1)
                dve.wait_ge(wd_taken, t + 1)
                dve.tensor_scalar(yd_tile(t), sq[:, 1], col("g_ffn_post", t), None, ALU.mult)

            for g in range(GROUPS):
                n = g * PER_GROUP
                for i in range(4):
                    both(n + 1 + i, (i + 1) % 2, 1 + i)
                    if g:
                        down_tile(g - 1, i)
                if g:
                    add_down_square(4 * g - 1)
                with dve.Fori(2, PER_GROUP // 2 - 1) as t:
                    both(t * 2 + (n + 1), 1, t * 2 + 1)
                    both(t * 2 + (n + 2), 0, t * 2 + 2)
                both(n + PER_GROUP - 1, 1, PER_GROUP - 1)
                if g < GROUPS - 1:
                    both(n + PER_GROUP, 0, 0)
            for t in range(KT - 4, KT):
                add_down_square(t)
            invert_root(6, rms[:], std)
            dve.wait_ge(x1_landed, 16 * KT)
            dve.wait_ge(yd_last_done, 4)
            for k in range(OUT_POOL, KT + 1):
                if k < KT:
                    dve.tensor_tensor(yd_tile(k), yd_tile(k), rms[:], ALU.mult).then_inc(yd_scaled, 1)
                if k > OUT_POOL:
                    dve.wait_ge(yd_scaled, k - OUT_POOL)
                    dve.tensor_tensor(x1_back[:, k - 1], x1_back[:, k - 1], yd_tile(k - 1), ALU.add).then_inc(
                        out_ready, 1)

        @block.tensor
        def _(pe):
            def product(dst, a, b, start, stop):
                (ah, al), (bh, bl) = a, b
                pe.matmul(dst, ah, bh, start=start, stop=False)
                pe.matmul(dst, ah, bl, start=False, stop=False)
                return pe.matmul(dst, al, bh, start=False, stop=stop)

            def w_tile(s, c):
                return w_hi[:, s, c * P:c * P + P], w_lo[:, s, c * P:c * P + P]

            def unit(u, s, half, bank, start, stop, each=None, middle=None):
                pe.wait_ge(split_done, u + 1)
                for i in range(UK):
                    k = half * UK + i
                    if each:
                        each(k)
                    if middle and i == UK // 2:
                        middle()
                    last = product(bank[:], w_tile(s, i), (act_hi[:, k], act_lo[:, k]),
                                   start and i == 0, stop and i == UK - 1)
                last.then_inc(unit_used, 1)

            def tile(u, bank, between=None, middle=None, middle2=None):
                unit(u, 0, 0, bank, True, False, middle=middle)
                if between:
                    between()
                unit(u + 1, 1, 1, bank, False, True, middle=middle2)

            def channel_sum(bank, *srcs):
                for i, src in enumerate(srcs):
                    last = pe.matmul(bank[:], ones[:], src, start=(i == 0), stop=(i == len(srcs) - 1))
                last.then_inc(sum_done, 1)

            def column_sum(bank, src):
                for j in range(QT):
                    last = pe.matmul(bank[:, j:j + 1], src[:, P * j:P * j + P], ones[:, 0:1], start=True, stop=True)
                last.then_inc(sum_done, 1)

            def spread(bank):
                pe.wait_ge(diag_done, 1)
                pe.matmul(bank[:], ones[:], sq[:, 0], start=True, stop=True).then_inc(spread_done, 1)

            def scores(n, e):
                h = slice(HD * e, HD * e + HD)
                for i, (qt, b, bc, _) in enumerate(S_SEGS):
                    q = slice(P * qt, P * qt + P)
                    keys = slice(0, P * (qt + 1))
                    last = product(SB[b][:, bc:bc + P * (qt + 1)], (q_hi[h, q], q_lo[h, q]),
                                   (k_hi[h, keys], k_lo[h, keys]), True, True)
                    if i != 1:
                        last.then_inc(qk_done, 1)

            def transposes(n, e):
                pe.wait_ge(probs_ready, n + 1)
                at_least(pe, pt_split, n * 3)
                for i, (j, b, bc, _) in enumerate(T_SEGS):
                    for qt in range(j, QT):
                        c = S_COL[qt] + P * j
                        last = pe.transpose(PT[b][:, bc + P * (qt - j):bc + P * (qt - j) + P], sm[:, c:c + P],
                                            ident[:])
                    if i != 1:
                        last.then_inc(pt_done, 1)

            def values(n, e):
                pe.wait_ge(pt_split, n * 3 + 3)
                for j in range(QT):
                    w = P * (QT - j)
                    pt = slice(T_COL[j], T_COL[j] + w)
                    last = product(PJ[e][:, P * j:S], (v_hi[:, j], v_lo[:, j]), (pt_hi[e][:, pt], pt_lo[e][:, pt]),
                                   j == 0, j == QT - 1)
                last.then_inc(pv_done, 1)

            def v_transposes(p):
                pe.wait_ge(v_taken, p)
                pe.wait_ge(g_taken, p)
                for j in range(QT):
                    last = pe.transpose(PJ[1][:, P * j:P * j + P], v_t[:, P * j:P * j + P], ident[:])
                last.then_inc(vt_done, 1)

            def attention_rest(p):
                pe.wait_ge(v_split, p)
                values(p * 2 - 2, 0)
                values(p * 2 - 1, 1)

            def pair(p, prev):
                u = p * PER_PAIR + U_MIX
                if prev:
                    pe.wait_ge(s_taken, p * 6)
                    tile(u, SB[0], lambda: v_transposes(p), lambda: transposes(p * 2 - 1, 1))
                else:
                    tile(u, SB[0])
                if prev:
                    attention_rest(p)
                    pe.wait_ge(gates_taken, p * 2)

                def x_sum():
                    pe.wait_ge(sq_added, KT // 2)
                    pe.wait_ge(sq_added_b, KT // 2)
                    channel_sum(SB[2], acc[:], acc_b[:])

                tile(u + 2, SB[1], middle=None if prev else x_sum)
                if prev:
                    pe.wait_ge(ya_taken, p * 2 - 1)
                else:
                    pe.wait_ge(f_taken, 1)
                tile(u + 4, PJ[0])
                pe.wait_ge(q_split, p + 1)
                pe.wait_ge(k_split, p + 1)
                scores(p * 2, 0)
                if prev:
                    pe.wait_ge(ya_taken, p * 2)

                def spread_negc():
                    pe.wait_ge(negc_ready, 1)
                    for e in range(2):
                        last = pe.matmul(PT[e][:], pick[0:2 * NP, e], tt[0:2 * NP], start=True, stop=True)
                    last.then_inc(negc_spread, 1)

                tile(u + 6, PJ[1], middle2=None if prev else spread_negc)
                transposes(p * 2, 0)
                pe.wait_ge(s_taken, p * 6 + 3)
                scores(p * 2 + 1, 1)
                pe.wait_ge(x_taken, p + 1)
                tile(u + 8, PJ[0])
                pe.wait_ge(s_taken, p * 6 + 6)
                pe.wait_ge(gw_split, p + 1)
                pe.wait_ge(xc_split, p + 1)
                for g in range(2):
                    last = product(SB[1 + g][:], (gw_hi[:, g], gw_lo[:, g]), (xc_hi[:], xc_lo[:]), True, True)
                last.then_inc(gates_done, 1)

            def after_split(n):
                return lambda k: pe.wait_ge(act_split, n + k + 1)

            unit(0, 0, 0, PJ[0], True, False, after_split(0))
            unit(1, 1, 1, PJ[0], False, True, after_split(0))
            pe.wait_ge(consts_set, 5)
            pair(0, False)
            with pe.Fori(1, NP) as p:
                pair(p, True)
            transposes(2 * NP - 1, 1)
            v_transposes(NP)
            attention_rest(NP)

            def y_split(k):
                if k in Y_POOL:
                    pe.wait_ge(rnn_split, Y_POOL.index(k) + 1)
                else:
                    pe.wait_ge(act_split, KT + Y_VECTOR.index(k) + 1)

            def out_tile(t, s, first=False):
                u = t * 2 + U_OUT
                a, b = ((SB[0], SB[1]), (PT[0], PT[1]))[s]
                unit(u, 0, 0, a, True, True, y_split if first else None)
                unit(u + 1, 1, 1, b, True, True, y_split if first else None)

            pe.wait_ge(s_taken, 6 * NP)
            pe.wait_ge(gates_taken, 2 * NP)
            out_tile(0, 0, True)
            pe.wait_ge(ynorm_ready, 2)
            channel_sum(SB[2], acc[:])
            channel_sum(PT[2], acc_b[:])
            out_tile(1, 1)
            with pe.Fori(1, KT // 2) as i:
                pe.wait_ge(wo_taken, i * 2 - 1)
                out_tile(i * 2, 0)
                pe.wait_ge(wo_taken, i * 2)
                out_tile(i * 2 + 1, 1)
            pe.wait_ge(osum_ready, 1)
            pe.wait_ge(std_done, 3)
            column_sum(SB[2], acc)
            spread(PT[2])

            pe.wait_ge(wo_taken, KT)
            for half in range(2):
                unit(U_FF + half, half, half, PT[0], half == 0, half == 1,
                     lambda k: pe.wait_ge(act_split, AFTER_Y + k + 1))

            def x1_sum():
                pe.wait_ge(x1sum_ready, KT // 2 - 1)
                pe.wait_ge(x1sum_b_ready, 1)
                channel_sum(SB[2], acc[:], rms_a[:])

            tile(U_FF + 2, PT[1], middle2=x1_sum)
            tile(U_FF + 4, PJ[0])
            tile(U_FF + 6, PJ[1])
            with pe.Fori(2, FT) as j:
                pe.wait_ge(gate_taken, j)
                tile(j * 4 + U_FF, PJ[0])
                pe.wait_ge(up_taken, j)
                tile(j * 4 + (U_FF + 2), PJ[1])

            def down_unit(n, s, out_banks, start=False, stop=False):
                pe.wait_ge(split_done, n + (U_DOWN + 1))
                pe.wait_ge(h_split, n + 1)
                for kt in range(2):
                    tok = slice(S * kt, S * kt + S)
                    for i, bank in enumerate(out_banks):
                        last = product(bank[:], w_tile(s, 4 * kt + i), (h_hi[s][:, tok], h_lo[s][:, tok]),
                                       start and kt == 0, stop and kt == 1)
                last.then_inc(unit_used, 1)

            pe.wait_ge(std_done, 5)
            for g in range(GROUPS):
                n, out_banks = g * PER_GROUP, DOWN_BANKS[g % 2]
                if g == 1:
                    pe.wait_ge(up_taken, FT)
                at_least(pe, wd_taken, 4 * (g - 1))
                down_unit(n, 0, out_banks, start=True)
                down_unit(n + 1, 1, out_banks)
                with pe.Fori(1, PER_GROUP // 2 - 1) as t:
                    down_unit(t * 2 + n, 0, out_banks)
                    down_unit(t * 2 + (n + 1), 1, out_banks)
                down_unit(n + PER_GROUP - 2, 0, out_banks)
                down_unit(n + PER_GROUP - 1, 1, out_banks, stop=True)
            pe.wait_ge(wdsum_ready, 1)
            channel_sum(SB[2], acc[:])


def kernel(x, norm_mix_pre, w_in, b_forget, conv_rnn_w, conv_rnn_b, w_rg_a, b_rg_a, w_rg_x, b_rg_x, rg_lambda,
           norm_attn_out, norm_rnn_out, w_out, norm_mix_post, norm_ffn_pre, w_gate, w_up, conv_ffn_w, conv_ffn_b,
           w_down, norm_ffn_post):
    import numpy as np
    import concourse.bacc as bacc
    from concourse.bass_utils import run_bass_kernel_spmd

    def tiles(v):
        return np.asarray(v).reshape(-1, P).T

    xT = np.ascontiguousarray(np.asarray(x)[0].T.reshape(KT, P, S).transpose(1, 0, 2))
    par = np.zeros((P, NPAR), np.float32)
    for name, v in (("g_pre", norm_mix_pre), ("conv_w", conv_rnn_w), ("conv_b", conv_rnn_b), ("b_a", b_rg_a),
                    ("b_x", b_rg_x), ("lam", rg_lambda), ("g_y", norm_attn_out), ("g_post", norm_mix_post),
                    ("g_ffn", norm_ffn_pre), ("ffn_w", conv_ffn_w), ("ffn_b", conv_ffn_b),
                    ("g_ffn_post", norm_ffn_post)):
        t = tiles(v)
        par[:, COLS[name]:COLS[name] + t.shape[1]] = t
    par[:, COLS["g_y"] + NP:COLS["g_y"] + KT] = tiles(norm_rnn_out)
    par[0:2 * NP, COLS["b_forget"]] = np.asarray(b_forget)[0]

    weights = np.zeros((NU, P, UW), np.float32)

    def units(w):
        w = np.asarray(w)
        return w.reshape(2, UK, P, -1, P).transpose(3, 0, 2, 1, 4).reshape(-1, 2, P, UW)

    win = np.asarray(w_in)[0]
    f0, x0 = 3 * DA, 3 * DA + 2 * NP
    weights[0:2].reshape(2, P, UK, P)[:, :, :, 0:2 * NP] = win[:, f0:x0].reshape(2, UK, P, 2 * NP).transpose(0, 2, 1, 3)
    mixed = weights[U_MIX:U_OUT].reshape(NP, 5, 2, P, UW)
    for i, c in enumerate((0, DA, x0, x0 + DA, 2 * DA)):
        mixed[:, i] = units(win[:, c:c + DA])
    weights[U_OUT:U_FF] = units(w_out[0]).reshape(-1, P, UW)
    hidden = weights[U_FF:U_DOWN].reshape(FT, 2, 2, P, UW)
    hidden[:, 0] = units(w_gate[0])
    hidden[:, 1] = units(w_up[0])
    weights[U_DOWN:] = np.asarray(w_down)[0].reshape(PER_GROUP, 2, P, GROUPS, 4 * P).transpose(3, 0, 2, 1, 4).reshape(
        -1, P, UW)

    gate_w = np.zeros((NP, P, 2, P), np.float32)
    for g, w in enumerate((w_rg_a, w_rg_x)):
        w = np.asarray(w)[0].reshape(NP, 2, HD, HD)
        for e in range(2):
            gate_w[:, HD * e:HD * e + HD, g, HD * e:HD * e + HD] = w[:, e]

    nc = bacc.Bacc("TRN2", target_bir_lowering=False, num_devices=1)
    arrays = {"xT": xT, "params": par, "weights": weights, "gate_w": gate_w}
    aps = [nc.dram_tensor(n, a.shape, F32, kind="ExternalInput").ap() for n, a in arrays.items()]
    out = nc.dram_tensor("out", (P, KT, S), F32, kind="ExternalOutput").ap()
    block_kernel(nc, *aps, out)
    r = run_bass_kernel_spmd(nc, [arrays], core_ids=[0])
    got = np.asarray(r.results[0]["out"])
    return np.ascontiguousarray(got.transpose(1, 0, 2).reshape(D, S).T)[None]
```
